# Optimizing a Trainium2 kernel written in Bass

```python
import math
import jax, jax.numpy as jnp
from jax import lax
import numpy as np

D_MODEL = 1024
BATCH = 1
SEQ = 1024
DEPTH = 1
DEC_BATCH = 8
DEC_SEQ = 1
PAST_LEN = 512
PAGE_SIZE = 128

N_HEADS = 8
HEAD_DIM = 64
D_ATTN = N_HEADS * 2 * HEAD_DIM
POOL_WINDOWS = (2, 4, 8, 16)
N_POOL_GROUPS = len(POOL_WINDOWS)
D_POOL = D_MODEL // 2
POOL_GROUP = D_POOL // N_POOL_GROUPS
POOL_BUF = max(POOL_WINDOWS) - 1
D_FF = 4 * D_MODEL
ROPE_THETA = 10000.0
Q_BLOCK = 128
RMS_EPS = 1e-6
SUBLN_EPS = 1e-5
NEG_INF = -1e30
OFF_Q = D_POOL
OFF_K = OFF_Q + D_ATTN
OFF_V = OFF_K + D_ATTN
OFF_G = OFF_V + D_ATTN
D_IN = OFF_G + 2 * D_MODEL

kernel_name = 'hybrid_pool_diffattn_decode_step'

def _lambda_init(layer):
    return 0.8 - 0.6 * math.exp(-0.3 * layer)

def _rms_norm(x, g, eps):
    xf = x.astype(jnp.float32)
    xf = xf * lax.rsqrt(jnp.mean(xf * xf, axis=-1, keepdims=True) + eps)
    return (xf * g.astype(jnp.float32)).astype(x.dtype)

def _rope(x, pos):
    half = HEAD_DIM // 2
    inv_freq = ROPE_THETA ** (-jnp.arange(half, dtype=jnp.float32) * (2.0 / HEAD_DIM))
    ang = pos.astype(jnp.float32)[:, None] * inv_freq[None, :]
    cos = jnp.cos(ang)[:, None, None, :]
    sin = jnp.sin(ang)[:, None, None, :]
    xf = x.astype(jnp.float32)
    x1, x2 = xf[..., :half], xf[..., half:]
    return jnp.concatenate([x1 * cos - x2 * sin, x1 * sin + x2 * cos], axis=-1).astype(x.dtype)

def _pool_mixer(u_full, pos, w_grp, scale):
    B, L, _ = u_full.shape
    T = pos.shape[0]
    uf = u_full.astype(jnp.float32)
    cz = jnp.concatenate([jnp.zeros((B, 1, D_POOL), jnp.float32), jnp.cumsum(uf, axis=1)], axis=1)
    outs = []
    for g, w in enumerate(POOL_WINDOWS):
        sl = slice(g * POOL_GROUP, (g + 1) * POOL_GROUP)
        cg = cz[..., sl]
        c_lag = jnp.concatenate([jnp.zeros((B, w, POOL_GROUP), jnp.float32), cg], axis=1)
        win = cg[:, L + 1 - T:] - c_lag[:, L + 1 - T:L + 1]
        count = jnp.minimum(pos + 1, w).astype(jnp.float32)[None, :, None]
        outs.append(win / count - uf[:, L - T:, sl])
    pooled = jnp.stack(outs, axis=2).astype(u_full.dtype)
    y = jnp.einsum('btgc,gcd->btgd', pooled, w_grp).reshape(B, T, D_POOL)
    return y * scale

def _diff_attend(q, k, v, mask, lam):
    s = jnp.einsum('bqhcd,bkhcd->bhcqk', q, k).astype(jnp.float32) * (HEAD_DIM ** -0.5)
    s = jnp.where(mask[None, None, None], s, NEG_INF)
    p = jax.nn.softmax(s, axis=-1)
    a = p[:, :, 0] - lam * p[:, :, 1]
    return jnp.einsum('bhqk,bkhe->bqhe', a.astype(v.dtype), v)

def _attend_prompt(q, k, v, lam):
    B, T = q.shape[:2]
    nblk = T // Q_BLOCK
    qb = q.reshape(B, nblk, Q_BLOCK, N_HEADS, 2, HEAD_DIM).swapaxes(0, 1)
    kpos = jnp.arange(T)

    def block(args):
        qi, i = args
        qpos = i * Q_BLOCK + jnp.arange(Q_BLOCK)
        return _diff_attend(qi, k, v, kpos[None, :] <= qpos[:, None], lam)

    o = lax.map(block, (qb, jnp.arange(nblk)))
    return o.swapaxes(0, 1).reshape(B, T, N_HEADS, 2 * HEAD_DIM)

def _attend_sample(q, k_new, v_new, cache_k, cache_v, page_table, layer, lam):
    Bd, T = q.shape[:2]
    past = page_table.shape[1] * PAGE_SIZE
    pk = cache_k[layer, page_table].reshape(Bd, past, N_HEADS, 2, HEAD_DIM)
    pv = cache_v[layer, page_table].reshape(Bd, past, N_HEADS, 2 * HEAD_DIM)
    k_all = jnp.concatenate([pk.astype(k_new.dtype), k_new], axis=1)
    v_all = jnp.concatenate([pv.astype(v_new.dtype), v_new], axis=1)
    mask = jnp.arange(past + T)[None, :] <= (past + jnp.arange(T))[:, None]
    return _diff_attend(q, k_all, v_all, mask, lam)

def _decoder_layer(x, pos, pool_prev, cache_k, cache_v, page_table, layer, p):
    B, T, _ = x.shape
    h = _rms_norm(x, p['g_mix'], RMS_EPS)
    z = h @ p['w_in']
    u = z[..., :OFF_Q]
    q = _rope(z[..., OFF_Q:OFF_K].reshape(B, T, N_HEADS, 2, HEAD_DIM), pos)
    k = _rope(z[..., OFF_K:OFF_V].reshape(B, T, N_HEADS, 2, HEAD_DIM), pos)
    v = z[..., OFF_V:OFF_G].reshape(B, T, N_HEADS, 2 * HEAD_DIM)
    gate_pool = jax.nn.sigmoid(z[..., OFF_G:OFF_G + D_MODEL])
    gate_attn = jax.nn.sigmoid(z[..., OFF_G + D_MODEL:])

    u_full = u if pool_prev is None else jnp.concatenate([pool_prev.astype(u.dtype), u], axis=1)
    pool_out = _pool_mixer(u_full, pos, p['w_pool_grp'], p['pool_scale'])
    new_pool = u_full[:, -POOL_BUF:]

    lam_init = _lambda_init(layer)
    lam = (jnp.exp(jnp.sum(p['lambda_q1'].astype(jnp.float32) * p['lambda_k1'].astype(jnp.float32)))
           - jnp.exp(jnp.sum(p['lambda_q2'].astype(jnp.float32) * p['lambda_k2'].astype(jnp.float32)))
           + lam_init)
    if cache_k is None:
        o = _attend_prompt(q, k, v, lam)
    else:
        o = _attend_sample(q, k, v, cache_k, cache_v, page_table, layer, lam)
    o = _rms_norm(o, p['g_subln'], SUBLN_EPS) * (1.0 - lam_init)

    merged = (gate_pool * (pool_out @ p['w_pool_proj'])
              + gate_attn * (o.reshape(B, T, D_ATTN) @ p['w_attn_proj']))
    x = x + merged @ p['w_o']
    h2 = _rms_norm(x, p['g_mlp'], RMS_EPS)
    x = x + jnp.square(jax.nn.relu(h2 @ p['w_up'])) @ p['w_down']
    k_rows = k.reshape(B, T, N_HEADS, 2 * HEAD_DIM)
    return x, k_rows, v, new_pool

def setup_inputs(seed: int = 0) -> dict:
    key = jax.random.key(seed)
    ks = jax.random.split(key, 24)
    f32 = jnp.float32

    def nrm(k, shape, scale):
        return jax.random.normal(k, shape, f32) * scale

    n_pages = PAST_LEN // PAGE_SIZE
    n_pool_pages = (DEC_BATCH * n_pages * 5) // 4
    page_table = jax.random.permutation(ks[5], n_pool_pages)[:DEC_BATCH * n_pages]
    page_table = page_table.reshape(DEC_BATCH, n_pages).astype(jnp.int32)
    return {
        'x_prompt': nrm(ks[0], (BATCH, SEQ, D_MODEL), 1.0),
        'x_sample': nrm(ks[1], (DEC_BATCH, DEC_SEQ, D_MODEL), 1.0),
        'state_pool': nrm(ks[2], (DEPTH, DEC_BATCH, POOL_BUF, D_POOL), 1.0),
        'cache_k': nrm(ks[3], (DEPTH, n_pool_pages, PAGE_SIZE, N_HEADS, 2 * HEAD_DIM), 1.0),
        'cache_v': nrm(ks[4], (DEPTH, n_pool_pages, PAGE_SIZE, N_HEADS, 2 * HEAD_DIM), 1.0),
        'page_table': page_table,
        'g_mix': 1.0 + nrm(ks[6], (DEPTH, D_MODEL), 0.05),
        'w_in': nrm(ks[7], (DEPTH, D_MODEL, D_IN), D_MODEL ** -0.5),
        'w_pool_grp': nrm(ks[8], (DEPTH, N_POOL_GROUPS, POOL_GROUP, POOL_GROUP), POOL_GROUP ** -0.5),
        'pool_scale': 1.0 + nrm(ks[9], (DEPTH, D_POOL), 0.1),
        'w_pool_proj': nrm(ks[10], (DEPTH, D_POOL, D_MODEL), D_POOL ** -0.5),
        'lambda_q1': nrm(ks[11], (DEPTH, HEAD_DIM), 0.1),
        'lambda_k1': nrm(ks[12], (DEPTH, HEAD_DIM), 0.1),
        'lambda_q2': nrm(ks[13], (DEPTH, HEAD_DIM), 0.1),
        'lambda_k2': nrm(ks[14], (DEPTH, HEAD_DIM), 0.1),
        'g_subln': 1.0 + nrm(ks[15], (DEPTH, 2 * HEAD_DIM), 0.05),
        'w_attn_proj': nrm(ks[16], (DEPTH, D_ATTN, D_MODEL), D_ATTN ** -0.5),
        'w_o': nrm(ks[17], (DEPTH, D_MODEL, D_MODEL), D_MODEL ** -0.5),
        'g_mlp': 1.0 + nrm(ks[18], (DEPTH, D_MODEL), 0.05),
        'w_up': nrm(ks[19], (DEPTH, D_MODEL, D_FF), D_MODEL ** -0.5),
        'w_down': nrm(ks[20], (DEPTH, D_FF, D_MODEL), D_FF ** -0.5),
        'g_final': 1.0 + nrm(ks[21], (D_MODEL,), 0.05),
    }

def reference(x_prompt, x_sample, state_pool, cache_k, cache_v, page_table,
              g_mix, w_in, w_pool_grp, pool_scale, w_pool_proj,
              lambda_q1, lambda_k1, lambda_q2, lambda_k2, g_subln,
              w_attn_proj, w_o, g_mlp, w_up, w_down, g_final):
    T_p = x_prompt.shape[1]
    T_s = x_sample.shape[1]
    past = page_table.shape[1] * PAGE_SIZE
    pos_prompt = jnp.arange(T_p, dtype=jnp.int32)
    pos_sample = past + jnp.arange(T_s, dtype=jnp.int32)
    xp, xs = x_prompt, x_sample
    kp_l, vp_l, pp_l, ks_l, vs_l, ps_l = [], [], [], [], [], []
    for layer in range(DEPTH):
        p = {
            'g_mix': g_mix[layer], 'w_in': w_in[layer], 'w_pool_grp': w_pool_grp[layer],
            'pool_scale': pool_scale[layer], 'w_pool_proj': w_pool_proj[layer],
            'lambda_q1': lambda_q1[layer], 'lambda_k1': lambda_k1[layer],
            'lambda_q2': lambda_q2[layer], 'lambda_k2': lambda_k2[layer],
            'g_subln': g_subln[layer], 'w_attn_proj': w_attn_proj[layer], 'w_o': w_o[layer],
            'g_mlp': g_mlp[layer], 'w_up': w_up[layer], 'w_down': w_down[layer],
        }
        xp, kp, vp, pp = _decoder_layer(xp, pos_prompt, None, None, None, None, layer, p)
        xs, kn, vn, pn = _decoder_layer(xs, pos_sample, state_pool[layer], cache_k, cache_v,
                                        page_table, layer, p)
        kp_l.append(kp); vp_l.append(vp); pp_l.append(pp)
        ks_l.append(kn); vs_l.append(vn); ps_l.append(pn)
    y_prompt = _rms_norm(xp, g_final, RMS_EPS)
    y_sample = _rms_norm(xs, g_final, RMS_EPS)
    new_k_prompt = jnp.stack(kp_l, axis=0)
    new_v_prompt = jnp.stack(vp_l, axis=0)
    new_pool_prompt = jnp.stack(pp_l, axis=0)
    new_k_sample = jnp.stack(ks_l, axis=0)
    new_v_sample = jnp.stack(vs_l, axis=0)
    new_pool_sample = jnp.stack(ps_l, axis=0)
    return (y_prompt, y_sample, new_k_prompt, new_v_prompt, new_pool_prompt,
            new_k_sample, new_v_sample, new_pool_sample)


_drawn_inputs = setup_inputs


def setup_inputs(seed=0):
    import zlib

    import numpy as np

    out = dict(_drawn_inputs(seed))
    spreads = {}
    factors = {'lambda_k2': 3.796, 'g_subln': 2.8}
    for name, (base, spread) in spreads.items():
        noise = np.random.default_rng([zlib.crc32(name.encode()), seed]).standard_normal(out[name].shape)
        drawn = base * np.exp(spread * noise) if base else spread * noise
        out[name] = __import__('jax').numpy.asarray(drawn.astype(out[name].dtype))
    for name, factor in factors.items():
        out[name] = (out[name] * factor).astype(out[name].dtype)
    return out
```

```python
from contextlib import ExitStack

import concourse.bass as bass
from concourse import mybir

ALU = mybir.AluOpType
ACT = mybir.ActivationFunctionType
AX_X = mybir.AxisListType.X
F32 = mybir.dt.float32
F32R = mybir.dt.float32r
BF16 = mybir.dt.bfloat16

P = 128
D = 1024
KT = D // P
SEQ = 1024
DEC = 8
TOK = SEQ + DEC
NTT = SEQ // P
NCH = 3
CH = TOK // NCH
HEADS = 8
HD = 64
HALF = HD // 2
DH = 2 * HD
FF = 4 * D
NG = 4
D_POOL = NG * P
WINDOWS = (2, 4, 8, 16)
BUF = 15
PAD = BUF + 1
PAGES = 4
PAST = PAGES * P
OFF_Q = D_POOL
OFF_K = OFF_Q + D
OFF_V = OFF_K + D
OFF_G = OFF_V + D
SCALE = HD ** -0.5
RMS_EPS = 1e-6
SUBLN_EPS = 1e-5
LAM_INIT = 0.8 - 0.6
ROUNDS = [0, 1, 2, 3, 4, 6, 8, 10, 12]
W_QKV = 4 * HEADS
RAW_QKV = 16 * HEADS
PART_A = [("u", 0), ("u", 1), ("grp", 0), ("u", 2), ("grp", 1), ("u", 3), ("grp", 2), ("gate", 0), ("grp", 3),
          ("pool", 0), ("gate", 1), ("pool", 1), ("gate", 2), ("pool", 2)]
N_A = 3
REDUCE_AT = (2, 4, 6, 8, 9, 10, 11, 12)
S_LOOP = len(PART_A)
L_LOOP = S_LOOP - NG
S_ATTN = S_LOOP + 2 * (KT - N_A)
S_OUT = S_ATTN + 2 * KT
S_MLP = S_OUT + KT
FG = FF // D
S_END = S_MLP + FG * 2 * KT
WQ = 4


def need(eng, sem, value):
    if isinstance(value, int) and value <= 0:
        return
    eng.wait_ge(sem, value)


def decoder_layer(nc, ins, outs):
    (x_prompt, x_sample, state_pool, cache_k, cache_v, page_table, g_mix, w_in, w_pool_grp, pool_scale,
     w_pool_proj, lambda_q1, lambda_k1, lambda_q2, lambda_k2, g_subln, w_attn_proj, w_o, g_mlp, w_up,
     w_down, g_final, c_cos, c_sin, c_ident, c_mask, c_cols, c_sel, c_eye8, c_inv) = ins
    (y_prompt, y_sample, new_k_p, new_v_p, new_pool_p, new_k_s, new_v_s, new_pool_s) = outs

    q_scr = nc.dram_tensor("q_sample_scratch", [DEC, D], F32, kind="Internal").ap()
    oT_scr = nc.dram_tensor("attention_out_scratch", [HEADS, P, SEQ], F32, kind="Internal").ap()

    xp = x_prompt.rearrange("b (t p) d -> p (b t) d", p=P)
    xs_ = x_sample.rearrange("b s d -> (b s) d")
    w_in0 = w_in[0].rearrange("(k p) n -> p k n", p=P)
    kp_out = new_k_p[0, 0].rearrange("(t p) h e -> p t h e", p=P)
    vp_out = new_v_p[0, 0].rearrange("(t p) h e -> p t h e", p=P)

    cursor = [(nc.sbuf_base + 31) // 32 * 32]

    def put(name, shape, dtype, at=None):
        size = 1
        for n in shape[1:]:
            size *= n
        size *= 2 if dtype == BF16 else 4
        off = cursor[0] if at is None else at
        t = nc.alloc_sbuf_tensor_at(name, shape, dtype, offset=off)
        end = (off + size + 31) // 32 * 32
        if at is None:
            cursor[0] = end
        return t, end

    ident, _ = put("ident", [P, P], F32)
    identb, _ = put("identb", [P, P], BF16)
    mask, _ = put("mask", [P, P], BF16)
    stat, _ = put("stat", [P, 64], F32)
    cols, _ = put("cols", [P, 32], F32)
    nlam, _ = put("nlam", [P, 1], F32)
    half_neg, _ = put("half_neg", [P, 64], F32)
    ones, _ = put("ones", [P, P], F32)
    pages, _ = put("pages", [1, DEC * PAGES], mybir.dt.int32)
    base_h = cursor[0]
    h_hi, _ = put("h_hi", [P, KT, TOK], F32R)
    h_lo, _ = put("h_lo", [P, KT, TOK], F32R)
    w_raw, _ = put("w_raw", [P, 3, KT, P], F32)
    w_hi, _ = put("w_hi", [P, 3, KT, P], F32R)
    w_lo, _ = put("w_lo", [P, 3, KT, P], F32R)
    base = cursor[0]

    kv_st, _ = put("kv_st", [P, 2, NTT + 1, 2, P], F32)
    qs_st, _ = put("qs_st", [P, 2, P], F32)
    q_nat, _ = put("q_nat", [P, P], F32)
    qk_hi, _ = put("qk_hi", [P, 2, 2, SEQ], F32R)
    qk_lo, _ = put("qk_lo", [P, 2, 2, SEQ], F32R)
    v_hl, _ = put("v_hl", [P, 2, NTT, 2, P], F32R)
    rope_c, _ = put("rope_c", [P, NTT + 1, HALF], F32)
    rope_s, _ = put("rope_s", [P, NTT + 1, HALF], F32)
    rc, _ = put("rc", [P, 2 * P], F32)
    rs, _ = put("rs", [P, 2 * P], F32)
    sums, _ = put("sums", [P, NTT, 2], F32)
    rsum, _ = put("rsum", [P, NTT, 2], F32)
    mx, _ = put("mx", [P, 2, 2], F32)
    nbias, _ = put("nbias", [P, 2, 2], F32)
    ratio, _ = put("ratio", [P, 2], F32)
    ssq, _ = put("ssq", [P, 2, NTT], F32)
    o_var, _ = put("o_var", [P, NTT], F32)
    o_rstd, _ = put("o_rstd", [P, NTT], F32)
    junk, _ = put("junk", [P, P], F32)
    o_low, _ = put("o_low", [P, P], F32)
    over = cursor[0]
    prob, _ = put("prob", [P, 2, 2, SEQ], F32)
    aT_hi, _ = put("aT_hi", [P, SEQ], F32R)
    aT_lo, _ = put("aT_lo", [P, SEQ], F32R)
    o_st, _ = put("o_st", [P, 2, NTT, P], F32)
    oT_st, _ = put("oT_st", [P, SEQ], F32)
    end_attn = cursor[0]
    x_in, a = put("x_in", [P, 3, D], F32, over)
    x_nrm, a = put("x_nrm", [P, 2, D], F32, a)
    g_bc, a = put("g_bc", [P, D], F32, a)
    x_junk, a = put("x_junk", [P, D], F32, a)
    lam_in, a = put("lam_in", [P, 4, HD], F32, a)
    lam_pr, a = put("lam_pr", [P, 2, HD], F32, a)
    mask_in, a = put("mask_in", [P, P], F32, a)
    assert a <= end_attn

    full = KT * TOK * 4
    r2, r3, r4, tmp = base, base + full, base + 2 * full, base + 3 * full
    slot2 = [t for t in (base - 3 * 3 * KT * P * 4 + i * 3 * KT * P * 4 + 2 * KT * P * 4 for i in range(3))]
    kv_pg, _ = put("kv_pages", [P, 2, PAGES, D], F32, r2)
    o_raw, _ = put("o_raw", [P, HEADS, TOK], F32, r2)
    o_lo, _ = put("o_lo", [P, HEADS, TOK], F32R, r2)
    x1, _ = put("x1", [P, KT, TOK], F32, r2)
    x1_chunks = x1.rearrange("p k (c n) -> p k c n", c=NCH)
    up, a = put("up", [P, PAD + TOK], F32, r3)
    win, a = put("win", [P, 2, PAD + SEQ], F32, a)
    pooled, a = put("pooled", [P, TOK], F32, a)
    pl_hi, a = put("pl_hi", [P, TOK], F32R, a)
    pl_lo, a = put("pl_lo", [P, TOK], F32R, a)
    assert a <= r4
    merged, _ = put("merged", [P, KT, TOK], F32, r3)
    h2_hi, _ = put("h2_hi", [P, KT, TOK], F32R, r3)
    y_hi, a = put("y_hi", [P, NG, TOK], F32R, r4)
    y_lo, a = put("y_lo", [P, NG, TOK], F32R, a)
    smp, _ = put("smp", [P, 4, D], F32, r4)
    o_hi, _ = put("o_hi", [P, HEADS, TOK], F32R, r4)
    h2_lo, _ = put("h2_lo", [P, KT, TOK], F32R, r4)
    mg_hi = nc.alloc_sbuf_tensor_at("mg_hi", [P, KT, TOK], F32R, offset=base_h)
    mg_lo = nc.alloc_sbuf_tensor_at("mg_lo", [P, KT, TOK], F32R, offset=base_h + full)
    ff_hi = nc.alloc_sbuf_tensor_at("ff_hi", [P, KT, TOK], F32R, offset=base_h)
    ff_lo = nc.alloc_sbuf_tensor_at("ff_lo", [P, KT, TOK], F32R, offset=base_h + full)
    q_bc = [put("q_bc0", [P, D], F32, slot2[1])[0], put("q_bc1", [P, D], F32, slot2[2])[0]]
    g_mlp_c = cols[:, 2:10]
    scale_c = cols[:, 10:14]
    gate, t0 = put("gate", [P, TOK], F32, tmp)
    wg_raw, a = put("wg_raw", [P, NG, P], F32, t0)
    wg_hi, a = put("wg_hi", [P, NG, P], F32R, a)
    wg_lo, a = put("wg_lo", [P, NG, P], F32R, a)
    a += D_POOL * 4
    inv_n, a = put("inv_n", [P, 16], F32, a)
    us, a = put("us", [P, NG, DEC, 16], F32, a)
    ufix, a = put("ufix", [P, 32], F32, a)
    tail_st, a = put("tail_st", [P, D_POOL], F32, slot2[0])
    state, a = put("state", [P, D_POOL], F32, a)
    a = ufix_end = t0 + 3 * 2048 + 2048 + 64 + 2048 + 128
    sc_all, a = put("sc_all", [P, PAGES, P], F32, a)
    sm_w, a = put("sm_w", [P, PAST], F32, a)
    a_all, a = put("a_all", [P, PAGES, DEC * HEADS], F32, a)
    a_one, a = put("a_one", [P, 2, PAGES, HEADS], F32, a)
    sel, a = put("sel", [P, DEC * HEADS], F32, a)
    eye8, a = put("eye8", [P, DEC], F32, a)
    own, a = put("own", [P, DEC, 16], F32, a)
    own_s, a = put("own_s", [P, 16], F32, a)
    ones_a, a = put("ones_a", [P, P], F32, a)
    vT, a = put("vT", [P, 64], F32, a)
    a_new, a = put("a_new", [P, 64], F32, a)
    o_s, a = put("o_s", [P, 4, 64], F32, a)
    dst, a = put("dst", [P, 32], F32, a)
    assert a <= nc.sbuf_usable_end, a - nc.sbuf_usable_end
    x_nat = [put(f"x_nat{i}", [P, NTT, P], F32, slot2[1 + i])[0] for i in range(2)]
    x_smp, _ = put("x_smp", [P, D], F32, slot2[0])
    xsT, a = put("xsT", [P, KT, DEC], F32, t0)
    sq, a = put("sq", [P, TOK], F32, a)
    xT, a = put("xT", [P, 2, TOK], F32, a)
    assert a <= nc.sbuf_usable_end, a - nc.sbuf_usable_end
    sq_sum, _ = put("sq_sum", [P, TOK], F32, tmp)
    r_bc, a = put("r_bc", [P, TOK], F32, t0)
    diag, a = put("diag", [P, NTT + 1, P], F32, a)
    hn, a = put("hn", [P, 2, TOK], F32, a)
    assert a <= nc.sbuf_usable_end
    relu, a = put("relu", [P, TOK], F32, t0)
    act_sq, a = put("act_sq", [P, TOK], F32, a)
    y_st, a = put("y_st", [P, 2, D], F32, t0)
    y_junk, a = put("y_junk", [P, D], F32, a)
    gf_bc, a = put("gf_bc", [P, D], F32, a)
    assert a <= nc.sbuf_usable_end

    with ExitStack() as ctx:
        ps = ctx.enter_context(nc.psum_tensor("ps", [P, 8, 512], F32))
        bank_z = ps[:, 0]
        bank_t = [ps[:, 1], ps[:, 6]]
        bank_s = ps[:, 2:6].rearrange("p (c b) n -> p c (b n)", c=2)
        bank_o = ps[:, 7]

        def sem(name):
            return ctx.enter_context(nc.semaphore(name))

        s_const = sem("const_in")
        s_x = [sem(f"x_in{i}") for i in range(3)]
        s_lam_pr, s_lam_sum, s_lam_exp, s_lam1, s_lam = [sem(f"lam_{n}") for n in ("pr", "sum", "exp", "dif", "ready")]
        s_half, s_mask = sem("half_ready"), sem("mask_ready")
        s_sq, s_var, s_rstd, s_xn = sem("x_sq"), sem("x_var"), sem("x_rstd"), sem("x_normed")
        s_ht, s_hhi, s_hlo = sem("hT_ready"), sem("h_hi_ready"), sem("h_lo_ready")
        s_raw = [sem(f"w_raw_in{i}") for i in range(3)]
        s_whi, s_wlo = sem("w_hi_ready"), sem("w_lo_ready")
        s_z, s_zfree, s_qk = sem("z_ready"), sem("z_free"), sem("qk_rotated")
        s_vhi, s_vlo = sem("v_hi_ready"), sem("v_lo_ready")
        s_qkt, s_qkhi, s_qklo = sem("qkT_ready"), sem("qk_hi_ready"), sem("qk_lo_ready")
        s_s, s_mx, s_nb, s_exp = sem("scores_ready"), sem("max_ready"), sem("bias_ready"), sem("exp_ready")
        s_rsum, s_ratio, s_a = sem("rsum_ready"), sem("ratio_ready"), sem("weights_ready")
        s_at, s_athi, s_atlo = sem("wT_ready"), sem("wT_hi_ready"), sem("wT_lo_ready")
        s_o, s_ol, s_oe, s_oq = sem("o_ready"), sem("o_low_out"), sem("o_out"), sem("o_squares")
        s_ovar, s_orstd, s_on = sem("o_var"), sem("o_rstd"), sem("o_normed")
        s_ont, s_one, s_ot = sem("onT_ready"), sem("onT_out"), sem("oT_stored")
        s_kv = [sem(f"kv_stored{i}") for i in range(2)]
        s_ones, s_tile, s_free = sem("ones_ready"), sem("product_ready"), [sem(f"product_out{i}") for i in range(2)]
        s_in2, s_smp, s_state, s_gf = sem("pool_consts_in"), sem("samples_in"), sem("state_in"), sem("g_final_in")
        s_pg = [sem(f"pages_in{i}") for i in range(2)]
        s_xin = [sem(f"x_cols_in{i}") for i in range(2)]
        s_xs = sem("x_samples_in")
        s_oraw = [sem(f"o_in{i}") for i in range(HEADS // 2)]
        s_pad, s_ust, s_us = sem("pad_ready"), sem("stateT_ready"), sem("stateT_out")
        s_osd, s_diag, s_rbc = sem("os_diag"), sem("diag_ready"), sem("r_bc_ready")
        s_prod2, s_vs, s_vp = sem("k_products_dve"), sem("v_steps"), sem("v_products")
        s_ufx = sem("sample_window")
        s_win, s_pooled, s_plhi, s_pllo, s_yhi = [sem(n) for n in ("window", "pooled", "pl_hi", "pl_lo", "y_hi")]
        s_tail, s_tailc, s_wghi, s_wglo = [sem(n) for n in ("tailT", "tail_out", "wg_hi", "wg_lo")]
        s_own, s_vt, s_vtc = sem("own_steps"), sem("vT_ready"), sem("vT_out")
        s_prod, s_kred, s_sct, s_soft, s_sexp = [sem(n) for n in ("k_products", "k_sums", "scoresT", "soft_steps",
                                                                  "sample_exp")]
        s_sela, s_vout, s_v, s_osq, s_oss, s_osv, s_osr, s_osmp = [sem(n) for n in (
            "sel_weights", "v_out", "v_ready", "os_steps", "os_sum", "os_var", "os_rstd", "os_ready")]
        s_ohi, s_olo, s_addm, s_mghi, s_mglo = [sem(n) for n in ("o_hi", "o_lo", "merged_added", "mg_hi", "mg_lo")]
        s_xt, s_xc, s_sqr, s_sqs = sem("xT_ready"), sem("xT_out"), sem("x1_squares"), sem("squares_added")
        s_n2, s_v2, s_r2, s_hn, s_h2hi, s_h2lo = [sem(n) for n in ("n2_sum", "n2_var", "n2_rstd", "hn_ready",
                                                                   "h2_hi", "h2_lo")]
        s_fsq, s_ffhi, s_fflo = sem("ff_squares"), sem("ff_hi"), sem("ff_lo")
        s_yt, s_ysq, s_yv, s_yr, s_yo = [sem(n) for n in ("yT", "y_squares", "y_var", "y_rstd", "y_ready")]
        s_yst = [sem(f"y_stored{i}") for i in range(2)]
        s_out = sem("pool_stored")

        block = ctx.enter_context(nc.Block())

        def rows(t):
            return P if t < NTT else DEC

        def toks(t):
            return slice(t * P, t * P + rows(t))

        def n_rounds(i):
            return 1 if i < 4 else 2

        N_CONST = 16 * 14

        PG_K = 16 * (PAGES + 1) * DEC // 2
        VS = 3

        def weighing(b, slot, g):
            part = kv_pg[:, slot, g:g + PAGES // 2].rearrange("p g (h e) -> p g h e", h=HEADS)
            w = a_all[:, g:g + PAGES // 2, bass.ds(b * HEADS, HEADS)]
            return part, part, w.unsqueeze(3).to_broadcast([P, PAGES // 2, HEADS, P])

        def psum_set(sp):
            return ps[:, 3 * sp:3 * sp + 3, 0:CH]

        def chunks(ap):
            return ap.rearrange("p (c n) -> p c n", c=NCH)

        def part_a():
            l = 0
            for s_, (kind, n) in enumerate(PART_A):
                yield s_, kind, n, (s_ // 2, s_ % 2, l // 2, l % 2)
                l += kind != "grp"

        def later(s_half, s_par):
            return s_half, s_par, s_half - NG // 2, s_par

        def gate_tile(i):
            return later(S_LOOP // 2 + i, 0)

        def pool_tile(i):
            return later(S_LOOP // 2 + i, 1)

        def ga_tile(n):
            return later(S_ATTN // 2 + n, 0)

        def ap_tile(n):
            return later(S_ATTN // 2 + n, 1)

        def out_tile(m, par):
            return later(S_OUT // 2 + m, par)

        def up_tile(g, j):
            return later(S_MLP // 2 + KT * g + j // 2, j % 2)

        def down_tile(g, n):
            return later(S_MLP // 2 + KT * g + KT // 2 + n // 2, n % 2)

        def tile_done(eng, t):
            eng.wait_ge(s_tile, 2 * t[0] + t[1] + 1)

        def tile_out(eng, t):
            eng.wait_ge(s_free[t[1]], t[0] + 1)

        def attention_done(eng):
            eng.wait_ge(s_one, 2 * HEADS)
            eng.wait_ge(s_ot, 16 * HEADS)
            for s_ in s_kv:
                eng.wait_ge(s_, 80 * HEADS // 2)

        @block.sync
        def _(sp):
            def load_x(t):
                if t >= 3:
                    sp.wait_ge(s_xn, t - 2)
                if t < NTT:
                    sp.dma_start(x_in[:, t % 3], xp[:, t]).then_inc(s_x[t % 3], 16)
                else:
                    sp.dma_start(x_in[0:DEC, t % 3], xs_).then_inc(s_x[t % 3], 16)

            def load_qkv(h):
                need(sp, s_wlo, WQ * h)
                for j, off in enumerate((OFF_Q, OFF_K, OFF_V)):
                    sp.dma_start(w_raw[:, j], w_in0[:, :, bass.ds(h * P + off, P)]).then_inc(s_raw[j], 16)

            def store_kv(h, par):
                sp.wait_ge(s_qk, 9 * h + 9)
                sp.wait_ge(s_zfree, 9 * h + 9)
                st = kv_st[:, par]
                sp.dma_start(kp_out[:, :, h], st[:, 0:NTT, 0]).then_inc(s_kv[par], 16)
                sp.dma_start(vp_out[:, :, h], st[:, 0:NTT, 1]).then_inc(s_kv[par], 16)
                sp.dma_start(new_k_s[0, :, 0, h], st[0:DEC, NTT, 0]).then_inc(s_kv[par], 16)
                sp.dma_start(new_v_s[0, :, 0, h], st[0:DEC, NTT, 1]).then_inc(s_kv[par], 16)
                sp.dma_start(q_scr[:, bass.ds(h * P, P)], qs_st[0:DEC, par]).then_inc(s_kv[par], 16)

            sp.dma_start(ident[:], c_ident).then_inc(s_const, 16)
            load_x(0)
            sp.dma_start(g_bc[:], g_mix[0:1].to_broadcast([P, D])).then_inc(s_const, 16)
            load_x(1)
            load_qkv(0)
            load_x(2)
            sp.dma_start(rope_c[:], c_cos).then_inc(s_const, 16)
            sp.dma_start(rope_s[:], c_sin).then_inc(s_const, 16)
            sp.dma_start(mask_in[:], c_mask).then_inc(s_const, 16)
            sp.dma_start(cols[:, 0:1], g_subln.rearrange("a e -> e a")).then_inc(s_const, 16)
            sp.dma_start(cols[:, 2:10], g_mlp[0].rearrange("(k p) -> p k", p=P),
                         allow_slow_non_contiguous=True).then_inc(s_const, 16)
            sp.dma_start(cols[:, 10:14], pool_scale[0].rearrange("(k p) -> p k", p=P),
                         allow_slow_non_contiguous=True).then_inc(s_const, 16)
            sp.dma_start(cols[:, 14:16], c_cols[:, 14:16]).then_inc(s_const, 16)
            sp.dma_start(pages[:], page_table.rearrange("(a b) g -> a (b g)", a=1)).then_inc(s_const, 16)
            for j, lam in enumerate((lambda_q1, lambda_k1, lambda_q2, lambda_k2)):
                sp.dma_start(lam_in[:, j], lam[0:1].to_broadcast([P, HD])).then_inc(s_const, 16)
            for t in range(3, NTT + 1):
                load_x(t)
            load_qkv(1)
            with sp.Fori(0, HEADS // 2 - 1) as p:
                for par in range(2):
                    store_kv(2 * p + par, par)
                    load_qkv(2 * p + par + 2)
            w_pool = w_pool_proj[0].rearrange("(k p) n -> p k n", p=P)
            w_attn = w_attn_proj[0].rearrange("(k p) n -> p k n", p=P)
            w_out = w_o[0].rearrange("(k p) n -> p k n", p=P)
            w_up0 = w_up[0].rearrange("(k p) n -> p k n", p=P)
            w_down0 = w_down[0].rearrange("(g k p) n -> p g k n", p=P, g=FG)
            sources = [(w_pool, NG, n) if kind == "pool" else (w_in0, KT, n + (OFF_G // P if kind == "gate" else 0))
                       for kind, n in PART_A if kind != "grp"]

            def load(lh, lp, src, kts, col):
                if not (isinstance(lh, int) and lh == 0):
                    sp.wait_ge(s_wlo, W_QKV + 2 * lh + lp - 1)
                sp.dma_start(w_raw[:, lp, 0:kts], src[:, :, bass.ds(col * P, P)]).then_inc(s_raw[lp], 16)

            def load_pages(b, slot, cache):
                for g in range(PAGES):
                    page = sp.value_load(pages[0:1, bass.ds(b * PAGES + g, 1)], min_val=0,
                                         max_val=cache_k.shape[1] - 1)
                    sp.dma_start(kv_pg[:, slot, g],
                                 cache[0, bass.ds(page, 1)].rearrange("a s h e -> s (a h e)")).then_inc(s_pg[slot], 16)

            def load_keys(b):
                need(sp, s_kred, b - 1)
                load_pages(b, b % 2, cache_k)
                sp.dma_start(q_bc[b % 2][:], q_scr[b:b + 1].to_broadcast([P, D])).then_inc(s_pg[b % 2], 16)

            def load_a(l):
                load(l // 2, l % 2, *sources[l])

            sp.wait_ge(s_const, N_CONST)
            store_kv(HEADS - 2, 0)
            sp.wait_ge(s_wlo, W_QKV)
            load_a(0)
            load_a(1)
            sp.dma_start(state[0:DEC * BUF], state_pool[0].rearrange("b r c -> (b r) c")).then_inc(s_state, 16)
            store_kv(HEADS - 1, 1)
            load_a(2)
            load_a(3)
            sp.dma_start(new_pool_s[0, :, 0:BUF - 1], state_pool[0, :, 1:BUF]).then_inc(s_out, 16)
            attention_done(sp)
            sp.dma_start(wg_raw[:], w_pool_grp[0].rearrange("g c d -> c g d")).then_inc(s_in2, 16)
            sp.dma_start(inv_n[:], c_inv).then_inc(s_in2, 16)
            sp.dma_start(sel[:], c_sel).then_inc(s_in2, 16)
            sp.dma_start(eye8[0:DEC], c_eye8).then_inc(s_in2, 16)
            sp.dma_start(smp[0:DEC, 0], q_scr).then_inc(s_smp, 16)
            sp.dma_start(smp[0:DEC, 1], new_k_s[0, :, 0].rearrange("b h e -> b (h e)")).then_inc(s_smp, 16)
            sp.dma_start(smp[0:DEC, 2], new_v_s[0, :, 0].rearrange("b h e -> b (h e)")).then_inc(s_smp, 16)
            load_keys(0)
            load_keys(1)
            n_gate = OFF_G // P
            lb = (S_LOOP - NG) // 2
            at = 0
            for l in range(4, 2 * lb):
                freed = [s_ for s_, kind, n, t in part_a() if 2 * t[2] + t[3] == l - 4 and kind != "grp"][0]
                while at < DEC - 2 and REDUCE_AT[at] < freed:
                    load_keys(at + 2)
                    at += 1
                load_a(l)
            for b in range(at + 2, DEC):
                load_keys(b)
            sp.wait_ge(s_tailc, 1)
            sp.dma_start(new_pool_p[0, 0], tail_st[0:BUF]).then_inc(s_out, 16)
            sp.dma_start(new_pool_s[0, :, BUF - 1], tail_st[BUF:BUF + DEC]).then_inc(s_out, 16)
            load(lb, 0, w_in0, KT, n_gate + N_A)
            sp.wait_ge(s_kred, DEC - 1)
            load_pages(0, 0, cache_v)
            load(lb, 1, w_pool, NG, N_A)
            sp.wait_ge(s_kred, DEC)
            load_pages(1, 1, cache_v)
            with sp.Fori(0, DEC // 2 - 1) as i:
                load(lb + 1 + i, 0, w_in0, KT, n_gate + N_A + 1 + i)
                load(lb + 1 + i, 1, w_pool, NG, N_A + 1 + i)
                for slot in range(2):
                    sp.wait_ge(s_v, 2 * i + slot + 1)
                    load_pages(2 * i + 2 + slot, slot, cache_v)
            sp.wait_ge(s_out, 48)
            sp.dma_start(x_smp[0:DEC], xs_).then_inc(s_xs, 16)
            for i in range(DEC // 2 - 1, KT - N_A - 1):
                load(lb + 1 + i, 0, w_in0, KT, n_gate + N_A + 1 + i)
                load(lb + 1 + i, 1, w_pool, NG, N_A + 1 + i)
            sp.wait_ge(s_v, DEC)
            for j in range(HEADS // 2):
                sp.dma_start(o_raw[:, 2 * j:2 * j + 2, 0:SEQ],
                             oT_scr[2 * j:2 * j + 2].rearrange("h e n -> e h n")).then_inc(s_oraw[j], 16)
            l0 = (S_ATTN - NG) // 2
            load(l0, 0, w_in0, KT, n_gate + KT)
            load(l0, 1, w_attn, KT, 0)
            with sp.Fori(1, KT) as n:
                load(l0 + n, 0, w_in0, KT, n_gate + KT + n)
                load(l0 + n, 1, w_attn, KT, n)
            with sp.Fori(0, KT // 2) as m:
                for par in range(2):
                    load((S_OUT - NG) // 2 + m, par, w_out, KT, 2 * m + par)
                    sp.wait_ge(s_xt, 2 * m + 1)
                    sp.dma_start(x_nat[par][:], xp[:, :, bass.ds((2 * m + par) * P, P)]).then_inc(s_xin[par], 16)
            with sp.Fori(0, FG) as g:
                for j in range(KT):
                    load((S_MLP - NG) // 2 + KT * g + j // 2, j % 2, w_up0, KT, KT * g + j)
                for n in range(KT):
                    lh = (S_MLP - NG) // 2 + KT * g + KT // 2 + n // 2
                    sp.wait_ge(s_wlo, W_QKV + 2 * lh + n % 2 - 1)
                    sp.dma_start(w_raw[:, n % 2], w_down0[:, bass.ds(g, 1), :, n * P:(n + 1) * P].rearrange(
                        "p a k n -> p (a k) n")).then_inc(s_raw[n % 2], 16)
            sp.dma_start(gf_bc[:], g_final.unsqueeze(0).to_broadcast([P, D])).then_inc(s_gf, 16)
            for t in range(NTT + 1):
                sp.wait_ge(s_yo, t + 1)
                if t < NTT:
                    sp.dma_start(y_prompt[0, t * P:(t + 1) * P], y_st[:, t % 2]).then_inc(s_yst[t % 2], 16)
                else:
                    sp.dma_start(y_sample.rearrange("b s d -> (b s) d"), y_st[0:DEC, t % 2]).then_inc(s_yst[t % 2], 16)
            sp.wait_ge(s_yst[0], 16 * 5)
            sp.wait_ge(s_yst[1], 16 * 4)
            sp.wait_ge(s_out, 48)

        @block.tensor
        def _(pe):
            def h_transposes(t):
                pe.wait_ge(s_xn, t + 1)
                n = rows(t)
                for r in range(2):
                    if r == 0:
                        need(pe, s_hlo, 2 * t - 1)
                    elif t >= 3:
                        pe.wait_ge(s_qklo, t - 2)
                    else:
                        need(pe, s_hlo, 2 * t)
                    for k in range(4):
                        kt = 4 * r + k
                        mm = pe.transpose(bank_t[r][:, k * n:(k + 1) * n],
                                          x_nrm[0:n, t % 2, kt * P:(kt + 1) * P], ident[0:n, 0:n])
                    mm.then_inc(s_ht, 1)

            def project(hp, t, half):
                n = rows(t)
                if half == 0:
                    need(pe, s_zfree, 9 * hp + t)
                for kt in range(4 * half, 4 * half + 4):
                    if t == 0 and kt % 2 == 0:
                        pe.wait_ge(s_wlo, WQ * hp + kt // 2 + 1)
                    for m, (a, w) in enumerate(((h_hi, w_hi), (h_hi, w_lo), (h_lo, w_hi))):
                        mm = pe.matmul(bank_z[0:n, 0:3 * P], a[:, kt, toks(t)], w[:, :, kt, :],
                                       start=(kt == 0 and m == 0), stop=(kt == KT - 1 and m == 2))
                if half == 1:
                    mm.then_inc(s_z, 1)

            def qk_transposes(hp, par, t):
                pe.wait_ge(s_qk, 9 * hp + t + 1)
                pe.transpose(bank_t[1][:, 0:P], q_nat[:], ident[:])
                pe.transpose(bank_t[1][:, P:2 * P], kv_st[:, par, t, 0], ident[:]).then_inc(s_qkt, 1)

            def scores(h, par, i):
                pe.wait_ge(s_qklo, 8 * h + i + 1)
                for c in range(2):
                    need(pe, s_exp, 16 * h + 2 * i + c - 1)
                    part = slice(HD * c, HD * c + HD)
                    for b in range(1 + i // 4):
                        n = min(512, (i + 1) * P - 512 * b)
                        out = bank_s[:, c, 512 * b:512 * b + n]
                        last = b == i // 4
                        for m, (q, k) in enumerate(((qk_hi, qk_hi), (qk_lo, qk_hi), (qk_hi, qk_lo))):
                            if m == 2 and b == i // 4:
                                pe.matmul(bank_s[:, c, i * P:(i + 1) * P], identb[:], mask[:],
                                          start=False, stop=False, skip_group_check=True)
                            mm = pe.matmul(out, q[part, par, 0, i * P:(i + 1) * P],
                                           k[part, par, 1, 512 * b:512 * b + n], start=(m == 0), stop=(m == 2))
                    mm.then_inc(s_s, 1)

            def weight_transposes(h, i, r, proj):
                if r == 0:
                    pe.wait_ge(s_a, 8 * h + i + 1)
                    need(pe, s_atlo, 12 * h - 1 if i == 0 else 12 * h + ROUNDS[i - 1] + 1)
                    if i == 3:
                        need(pe, s_one, 2 * h)
                elif proj:
                    pe.wait_ge(s_qklo, 8 * (h + 1) + i + 1)
                elif i == 4:
                    pe.wait_ge(s_one, 2 * h - 1)
                else:
                    pe.wait_ge(s_atlo, 12 * h + ROUNDS[i - 1] + 2)
                blocks = range(4 * r, min(4 * r + 4, i + 1))
                for k in blocks:
                    mm = pe.transpose(bank_t[r][:, (k - 4 * r) * P:(k - 4 * r + 1) * P],
                                      prob[:, i % 2, 0, k * P:(k + 1) * P], ident[:])
                mm.then_inc(s_at, 1)

            def values(h, par, i):
                pe.wait_ge(s_atlo, 12 * h + ROUNDS[i + 1])
                pe.wait_ge(s_vlo, 8 * h + i + 1)
                need(pe, s_oe, 8 * h + i)
                for k in range(i + 1):
                    for m, a in enumerate((aT_hi, aT_lo)):
                        mm = pe.matmul(bank_o[:, 0:2 * P], a[:, k * P:(k + 1) * P],
                                       v_hl[:, par, k].rearrange("p s e -> p (s e)"),
                                       start=(k == 0 and m == 0), stop=(k == i and m == 1))
                mm.then_inc(s_o, 1)

            def out_transposes(h, par, r, banks):
                if r == 0:
                    pe.wait_ge(s_on, h + 1)
                for t in range(4 * r, 4 * r + 4):
                    mm = pe.transpose(banks[r][:, (t - 4 * r) * P:(t - 4 * r + 1) * P],
                                      o_st[:, par, t], ident[:])
                mm.then_inc(s_ont, 1)

            def head(h, par, proj, normed):
                def turn_qk(t):
                    if t == 0:
                        need(pe, s_atlo, 12 * h)
                    elif t >= 5:
                        pe.wait_ge(s_atlo, 12 * h + ROUNDS[t - 1] + 2)
                    else:
                        pe.wait_ge(s_qklo, 8 * (h + 1) + t)
                    if t == 3 and normed:
                        pe.wait_ge(s_one, 2 * h - 1)
                    qk_transposes(h + 1, 1 - par, t)

                for s in range(NTT + 1):
                    if s < NTT:
                        scores(h, par, s)
                    if 2 <= s < NTT:
                        values(h, par, s - 2)
                    elif s == 0 and normed:
                        values(h - 1, 1 - par, NTT - 1)
                    if proj:
                        project(h + 1, s, 0)
                    if s == NTT:
                        values(h, par, s - 2)
                    if s >= 1:
                        weight_transposes(h, s - 1, 0, proj)
                        if proj:
                            turn_qk(s - 1)
                    if proj:
                        project(h + 1, s, 1)
                    if s >= 5:
                        weight_transposes(h, s - 1, 1, proj)
                    if normed and s == 3:
                        if proj:
                            pe.wait_ge(s_qklo, 8 * (h + 1) + 3)
                        else:
                            pe.wait_ge(s_atlo, 12 * h)
                        out_transposes(h - 1, 1 - par, 0, bank_t[::-1])
                        pe.wait_ge(s_atlo, 12 * h + ROUNDS[2] + 1)
                        out_transposes(h - 1, 1 - par, 1, bank_t[::-1])

            pe.wait_ge(s_const, N_CONST)
            for t in range(NTT + 2):
                if t <= NTT:
                    h_transposes(t)
                if t >= 1:
                    pe.wait_ge(s_hlo, 2 * t)
                    project(0, t - 1, 0)
                    project(0, t - 1, 1)
                if t >= 2:
                    if t <= NTT:
                        pe.wait_ge(s_hlo, 2 * t + 2)
                    else:
                        pe.wait_ge(s_qklo, t - 2)
                    qk_transposes(0, 0, t - 2)
            pe.wait_ge(s_mask, 1)
            head(0, 0, True, False)
            with pe.Fori(0, HEADS // 2 - 1) as p:
                head(2 * p + 1, 1, True, True)
                head(2 * p + 2, 0, True, True)
            head(HEADS - 1, 1, False, True)
            last = HEADS - 1
            values(last, 1, NTT - 1)

            def product(t, a_hi, a_lo, kts, ready=None, r0=1, between=None):
                sh, sp, lh, lp = t
                pe.wait_ge(s_wlo, W_QKV + 2 * lh + lp + 1)
                need(pe, s_free[sp], sh)
                for kt in range(kts):
                    if ready is not None:
                        pe.wait_ge(ready, kt + r0)
                    passes(sp, w_hi[:, lp, kt], w_lo[:, lp, kt], a_hi[:, kt], a_lo[:, kt], kt == 0, kt == kts - 1)
                    if between and kt in between:
                        between[kt]()

            def passes(sp, wh, wl, ah, al, first, last):
                for m, (w, a) in enumerate(((wh, ah), (wh, al), (wl, ah))):
                    for c in range(NCH):
                        mm = pe.matmul(ps[:, 3 * sp + c, 0:CH], w, a[:, c * CH:(c + 1) * CH],
                                       start=(first and m == 0), stop=(last and m == 2))
                if last:
                    mm.then_inc(s_tile, 1)

            def last_head_out():
                out_transposes(last, 1, 0, (ps[:, 6], ps[:, 7]))
                out_transposes(last, 1, 1, (ps[:, 6], ps[:, 7]))

            def state_transposes():
                pe.wait_ge(s_state, 16)
                pe.wait_ge(s_one, 2 * HEADS)
                n = DEC * BUF
                for g in range(NG):
                    mm = pe.transpose(ps[:, 6, g * n:(g + 1) * n], state[0:n, g * P:(g + 1) * P], ident[0:n, 0:n])
                mm.then_inc(s_ust, 1)

            def own_transposes():
                pe.wait_ge(s_smp, 48)
                for h in range(HEADS):
                    pe.transpose(bank_o[:, h * DEC:(h + 1) * DEC], smp[0:DEC, 2, h * P:(h + 1) * P],
                                 ident[0:DEC, 0:DEC])
                pe.wait_ge(s_own, 3)
                pe.wait_ge(s_ones, 1)
                pe.matmul(bank_o[:, 64:65], own[0:DEC].rearrange("p b m -> p (b m)"), ones[0:DEC, 0:1], start=True,
                          stop=True).then_inc(s_vt, 1)

            def tail_transpose(g):
                pe.wait_ge(s_free[(0, 1, 1, 1)[g]], (1, 1, 2, 3)[g])
                if g == 0:
                    pe.wait_ge(s_vtc, 1)
                n = BUF + DEC
                pe.transpose(bank_o[0:n, g * P:(g + 1) * P], up[:, PAD + TOK - n:PAD + TOK], ident[:]).then_inc(s_tail, 1)

            def score_transposes():
                pe.wait_ge(s_kred, DEC)
                pe.wait_ge(s_us, 1)
                for g in range(PAGES):
                    mm = pe.transpose(ps[:, 6, g * P:(g + 1) * P], sc_all[:, g], ident[:])
                mm.then_inc(s_sct, 1)

            def select_weights():
                pe.wait_ge(s_soft, 9)
                pe.wait_ge(s_tailc, 1)
                for g in range(PAGES):
                    pe.matmul(bank_o[:, g * 64:(g + 1) * 64], sm_w[:, g * P:(g + 1) * P], sel[:], start=True, stop=True)
                pe.matmul(bank_o[:, 256:320], ones_a[:], sel[:], start=True, stop=True).then_inc(s_sela, 1)

            def cached_values(i, slot):
                pe.wait_ge(s_vs, VS * (2 * i + slot + 1))
                for h in range(HEADS):
                    mm = pe.matmul(ps[:, 6, bass.ds((2 * i + slot) * HEADS + h, 1)], kv_pg[:, slot, 0, h * P:(h + 1) * P],
                                   ones[:, 0:1], start=True, stop=True)
                mm.then_inc(s_v, 1)

            pe.wait_ge(s_exp, 16 * HEADS)
            pe.wait_ge(s_atlo, 12 * HEADS)
            for s_, kind, n, t in part_a():
                if kind in ("u", "gate"):
                    product(t, h_hi, h_lo, KT, between={5: last_head_out} if s_ == 0 else None)
                elif kind == "grp":
                    tail_transpose(n)
                    pe.wait_ge(s_pllo, n + 1)
                    pe.wait_ge(s_wglo, 1)
                    need(pe, s_free[t[1]], t[0])
                    passes(t[1], wg_hi[:, n], wg_lo[:, n], pl_hi, pl_lo, True, True)
                else:
                    product(t, y_hi, y_lo, NG, s_free[0] if n == 0 else None, 2)
                if s_ == 0:
                    state_transposes()
                if s_ == 1:
                    own_transposes()
                if s_ == S_LOOP - 2:
                    score_transposes()
                if s_ == S_LOOP - 1:
                    select_weights()
            pe.wait_ge(s_vout, 2)
            with pe.Fori(0, DEC // 2) as i:
                product(gate_tile(i), h_hi, h_lo, KT)
                cached_values(i, 0)
                product(pool_tile(i), y_hi, y_lo, NG)
                cached_values(i, 1)
            for i in range(DEC // 2, KT - N_A):
                product(gate_tile(i), h_hi, h_lo, KT)
                product(pool_tile(i), y_hi, y_lo, NG)
            n_bh = DEC * HEADS

            def sample_norms():
                pe.wait_ge(s_osq, 3)
                pe.matmul(bank_o[0:n_bh, 0:1], o_s[:, 2], ones[:, 0:1], start=True, stop=True).then_inc(s_oss, 1)

            def spread_norms():
                pe.wait_ge(s_osd, 1)
                pe.matmul(bank_o[:, 64:64 + n_bh], ones[0:n_bh], o_s[0:n_bh, 3], start=True, stop=True).then_inc(s_oss, 1)
                pe.wait_ge(s_xs, 16)
                for k in range(KT):
                    mm = pe.transpose(ps[:, 6, k * DEC:(k + 1) * DEC], x_smp[0:DEC, k * P:(k + 1) * P],
                                      ident[0:DEC, 0:DEC])
                mm.then_inc(s_xt, 1)

            product(ga_tile(0), h_hi, h_lo, KT, between={0: sample_norms, 3: spread_norms})
            product(ap_tile(0), o_hi, o_lo, KT, s_olo)
            with pe.Fori(1, KT) as n:
                product(ga_tile(n), h_hi, h_lo, KT)
                product(ap_tile(n), o_hi, o_lo, KT, s_olo)
            with pe.Fori(0, KT // 2) as m:
                for par in range(2):
                    pe.wait_ge(s_xin[par], 16 * m + 16)
                    pe.wait_ge(s_xc, 2 * m + par + 1)
                    for k in range(NTT):
                        mm = pe.transpose(ps[:, 6 + k // 4, k % 4 * P:(k % 4 + 1) * P], x_nat[par][:, k], ident[:])
                    mm.then_inc(s_xt, 1)
                    product(out_tile(m, par), mg_hi, mg_lo, KT, s_mglo)
            pe.wait_ge(s_sqs, KT + 1)
            pe.wait_ge(s_free[0], S_MLP // 2)
            for t in range(NTT + 1):
                mm = pe.matmul(ps[0:rows(t), 0, t:t + 1], sq_sum[:, toks(t)], ones[:, 0:1], start=True, stop=True)
            mm.then_inc(s_n2, 1)
            pe.wait_ge(s_diag, 1)
            pe.wait_ge(s_xc, KT + 1)
            for t in range(NTT):
                pe.matmul(ps[:, 6 + t // 4, t % 4 * P:(t % 4 + 1) * P], ones[:], diag[:, t], start=True, stop=True)
            pe.matmul(ps[:, 0, 64:64 + DEC], ones[0:DEC], diag[0:DEC, NTT, 0:DEC], start=True, stop=True).then_inc(s_n2, 1)
            with pe.Fori(0, FG) as g:
                for j in range(KT):
                    product(up_tile(g, j), h2_hi, h2_lo, KT, s_h2lo if j == 0 else None)
                for n in range(KT):
                    sh, sp, lh, lp = down_tile(g, n)
                    pe.wait_ge(s_wlo, W_QKV + 2 * lh + lp + 1)
                    pe.wait_ge(s_free[sp], sh)
                    for kt in range(KT):
                        if n == 0:
                            pe.wait_ge(s_fflo, KT * g + kt + 1)
                        passes(sp, w_hi[:, lp, kt], w_lo[:, lp, kt], ff_hi[:, kt], ff_lo[:, kt], kt == 0, kt == KT - 1)
            for sp in range(2):
                pe.wait_ge(s_free[sp], S_END // 2)
            for t in range(NTT + 1):
                need(pe, s_yo, t - 3)
                for k in range(KT):
                    mm = pe.transpose(ps[0:rows(t), 2 * (t % 4) + k // 4, k % 4 * P:(k % 4 + 1) * P],
                                      x1[:, k, toks(t)], ident[:])
                mm.then_inc(s_yt, 1)

        @block.scalar
        def _(act):
            def split_qkv(hn):
                for j in range(3):
                    act.wait_ge(s_raw[j], 16 * hn + 16)
                need(act, s_z, 9 * hn)
                for q in range(WQ):
                    part = slice(2 * q, 2 * q + 2)
                    act.activation(w_hi[:, :, part], w_raw[:, :, part], ACT.Copy).then_inc(s_whi, 1)

            def square_x(t):
                n = rows(t)
                act.wait_ge(s_x[t % 3], 16 * (t // 3) + 16)
                need(act, s_sq, t)
                act.activation(x_junk[0:n], x_in[0:n, t % 3], ACT.Square,
                               accum_out=stat[0:n, t:t + 1]).then_inc(s_sq, 1)

            def h_high(t):
                n = rows(t)
                for r in range(2):
                    act.wait_ge(s_ht, 2 * t + r + 1)
                    act.activation(h_hi[:, 4 * r:4 * r + 4, toks(t)],
                                   bank_t[r][:, 0:4 * n].rearrange("p (k n) -> p k n", k=4), ACT.Copy).then_inc(s_hhi, 1)

            def qk_high(hp, par, t):
                act.wait_ge(s_qkt, 8 * hp + t + 1)
                act.activation(qk_hi[:, par, :, toks(t)], bank_t[1][:, 0:2 * P].rearrange("p (j n) -> p j n", j=2),
                               ACT.Copy).then_inc(s_qkhi, 1)

            def v_high(hp, par, t):
                act.wait_ge(s_zfree, 9 * hp + t + 1)
                act.activation(v_hl[:, par, t, 0], kv_st[:, par, t, 1], ACT.Copy).then_inc(s_vhi, 1)

            def exps(h, i, c):
                act.wait_ge(s_nb, 16 * h + 2 * i + c + 1)
                need(act, s_at, 12 * h + (ROUNDS[i - 1] if i else -2))
                n = (i + 1) * P
                act.activation(prob[:, i % 2, c, 0:n], bank_s[:, c, 0:n], ACT.Exp, bias=nbias[:, i % 2, c:c + 1],
                               scale=SCALE, accum_out=sums[:, i, c:c + 1]).then_inc(s_exp, 1)

            def weight_high(h, i, r):
                act.wait_ge(s_at, 12 * h + ROUNDS[i] + r + 1)
                need(act, s_o, 8 * h + i)
                n = min(512, (i + 1) * P - 512 * r)
                act.activation(aT_hi[:, 512 * r:512 * r + n], bank_t[r][:, 0:n], ACT.Copy).then_inc(s_athi, 1)

            def o_out(h, par, i):
                act.wait_ge(s_o, 8 * h + i + 1)
                need(act, s_oe, 8 * h + i)
                act.activation(o_low[:], bank_o[:, P:2 * P], ACT.Copy, scale=rsum[:, i, 0:1]).then_inc(s_ol, 1)

            def o_squares(h, par, i):
                act.wait_ge(s_oe, 8 * h + i + 1)
                need(act, s_oq, 8 * h + i)
                act.activation(junk[:], o_st[:, par, i], ACT.Square, accum_out=ssq[:, par, i:i + 1]).then_inc(s_oq, 1)

            def on_out(h, r, banks=bank_t[::-1]):
                act.wait_ge(s_ont, 2 * h + r + 1)
                if r == 0:
                    need(act, s_ot, 16 * h)
                act.activation(oT_st[:, 512 * r:512 * r + 512], banks[r][:, 0:512], ACT.Copy,
                               scale=cols[:, 1:2]).then_inc(s_one, 1)
                if r == 1:
                    act.wait_ge(s_one, 2 * h + 2)
                    act.dma_start(oT_scr[bass.ds(h, 1)].rearrange("a e n -> e (a n)"), oT_st[:]).then_inc(s_ot, 16)

            def head(h, par, proj, normed):
                if proj:
                    split_qkv(h + 1)
                for s in range(NTT + 1):
                    if s < NTT:
                        exps(h, s, 0)
                        exps(h, s, 1)
                    if s >= 2:
                        o_out(h, par, s - 2)
                    elif s == 0 and normed:
                        o_out(h - 1, 1 - par, NTT - 1)
                    if s >= 1:
                        weight_high(h, s - 1, 0)
                        if proj:
                            qk_high(h + 1, 1 - par, s - 1)
                    if s >= 2:
                        o_squares(h, par, s - 2)
                    elif s == 0 and normed:
                        o_squares(h - 1, 1 - par, NTT - 1)
                    if proj and s < NTT:
                        v_high(h + 1, 1 - par, s)
                    if s >= 5:
                        weight_high(h, s - 1, 1)
                    if normed and s == 3:
                        on_out(h - 1, 0)
                        on_out(h - 1, 1)

            split_qkv(0)
            act.wait_ge(s_const, N_CONST)
            act.wait_ge(s_lam_sum, 1)
            act.activation(stat[:, 34:36], stat[:, 32:34], ACT.Exp).then_inc(s_lam_exp, 1)
            act.activation(cols[:, 1:2], cols[:, 0:1], ACT.Copy, scale=1.0 - LAM_INIT)
            square_x(0)
            square_x(1)
            for t in range(NTT + 4):
                if t + 2 <= NTT:
                    square_x(t + 2)
                if t <= NTT:
                    h_high(t)
                if 1 <= t <= NTT:
                    v_high(0, 0, t - 1)
                if 2 <= t < NTT + 2:
                    qk_high(0, 0, t - 2)
            head(0, 0, True, False)
            with act.Fori(0, HEADS // 2 - 1) as p:
                head(2 * p + 1, 1, True, True)
                head(2 * p + 2, 0, True, True)

            def high(l):
                act.wait_ge(s_raw[l], RAW_QKV + 16)
                act.wait_ge(s_z, (NTT + 1) * HEADS)
                act.activation(w_hi[:, l], w_raw[:, l], ACT.Copy).then_inc(s_whi, 1)

            def next_high(t):
                sh, sp, lh, lp = t
                act.wait_ge(s_raw[lp], RAW_QKV + 16 * (lh + 2))
                tile_done(act, t)
                act.activation(w_hi[:, lp], w_raw[:, lp], ACT.Copy).then_inc(s_whi, 1)

            def sigmoid(t):
                tile_done(act, t)
                act.activation(chunks(gate), psum_set(t[1]), ACT.Sigmoid).then_inc(s_free[t[1]], 1)

            high(0)
            high(1)
            head(HEADS - 1, 1, False, True)
            o_out(HEADS - 1, 1, NTT - 1)
            o_squares(HEADS - 1, 1, NTT - 1)
            on_out(HEADS - 1, 0, (ps[:, 6], ps[:, 7]))
            on_out(HEADS - 1, 1, (ps[:, 6], ps[:, 7]))
            attention_done(act)
            act.wait_ge(s_pad, 1)

            def pooled_high(g):
                act.wait_ge(s_pooled, g + 1)
                act.activation(pl_hi[:], pooled[:], ACT.Copy).then_inc(s_plhi, 1)

            last_pool = None
            for s_, kind, n, t in part_a():
                if kind == "u":
                    tile_done(act, t)
                    if n:
                        act.wait_ge(s_tail, n)
                        act.wait_ge(s_pooled, n)
                    act.activation(chunks(up[:, PAD:PAD + TOK]), psum_set(t[1]), ACT.Copy).then_inc(s_free[t[1]], 1)
                    next_high(t)
                    if n == 0:
                        act.wait_ge(s_in2, 64)
                        act.activation(wg_hi[:], wg_raw[:], ACT.Copy).then_inc(s_wghi, 1)
                        pooled_high(0)
                        act.wait_ge(s_vt, 1)
                        act.activation(vT[:], bank_o[:, 0:64], ACT.Copy)
                        act.activation(dst[:, 8:9], bank_o[:, 64:65], ACT.Copy).then_inc(s_vtc, 1)
                elif kind == "grp":
                    tile_done(act, t)
                    act.activation(chunks(y_hi[:, n]), psum_set(t[1]), ACT.Copy, scale=scale_c[:, n:n + 1]).then_inc(s_yhi, 1)
                    if n < NG - 1:
                        pooled_high(n + 1)
                    else:
                        act.wait_ge(s_tail, NG)
                        act.activation(tail_st[0:BUF + DEC], bank_o[0:BUF + DEC, 0:D_POOL], ACT.Copy).then_inc(s_tailc, 1)
                elif kind == "gate":
                    if last_pool is not None:
                        tile_out(act, last_pool)
                    sigmoid(t)
                    next_high(t)
                else:
                    last_pool = t
                    next_high(t)
                if s_ == S_LOOP - 2:
                    act.wait_ge(s_soft, 3)
                    act.activation(sm_w[:], ps[:, 6], ACT.Exp, bias=dst[:, 2:3], scale=SCALE, accum_out=dst[:, 3:4])
                    act.activation(dst[:, 4:5], dst[:, 8:9], ACT.Exp, bias=dst[:, 2:3], scale=SCALE).then_inc(s_sexp, 1)
            act.wait_ge(s_sela, 1)
            act.activation(a_all.rearrange("p g m -> p (g m)"), bank_o[:, 0:256], ACT.Copy).then_inc(s_vout, 1)
            act.activation(a_new[:], bank_o[:, 256:320], ACT.Copy).then_inc(s_vout, 1)
            with act.Fori(0, KT - N_A) as i:
                act.wait_ge(s_free[1], S_LOOP // 2 + i)
                sigmoid(gate_tile(i))
                next_high(gate_tile(i))
                next_high(pool_tile(i))
            act.wait_ge(s_osmp, 1)
            act.wait_ge(s_xt, 1)
            act.activation(xsT.rearrange("p k b -> p (k b)"), ps[:, 6, 0:64], ACT.Copy).then_inc(s_xc, 1)
            for h in range(HEADS):
                act.wait_ge(s_oraw[h // 2], 16)
                act.activation(o_hi[:, h], o_raw[:, h], ACT.Copy).then_inc(s_ohi, 1)

            def merged_high(n):
                act.wait_ge(s_addm, n + 1)
                act.activation(mg_hi[:, n], merged[:, n], ACT.Copy).then_inc(s_mghi, 1)

            tile_out(act, pool_tile(KT - N_A - 1))
            sigmoid(ga_tile(0))
            next_high(ga_tile(0))
            next_high(ap_tile(0))
            with act.Fori(1, KT - 1) as n:
                act.wait_ge(s_addm, n)
                sigmoid(ga_tile(n))
                next_high(ga_tile(n))
                next_high(ap_tile(n))
            act.wait_ge(s_addm, KT - 1)
            sigmoid(ga_tile(KT - 1))
            next_high(ga_tile(KT - 1))
            for n in range(KT - 1):
                merged_high(n)
            next_high(ap_tile(KT - 1))
            merged_high(KT - 1)

            with act.Fori(0, KT // 2) as m:
                for par in range(2):
                    n = 2 * m + par
                    act.wait_ge(s_xt, n + 2)
                    act.wait_ge(s_xc, n + 1)
                    act.wait_ge(s_sqs, n + 1)
                    act.activation(xT[:, par, 0:SEQ].rearrange("p (b n) -> p b n", b=2), ps[:, 6:8], ACT.Copy)
                    act.activation(xT[:, par, SEQ:TOK].unsqueeze(1), xsT[:, bass.ds(n, 1)], ACT.Copy).then_inc(s_xc, 1)
                    tile_out(act, out_tile(m, par))
                    next_high(out_tile(m, par))
                    act.activation(sq[:].unsqueeze(1), x1[:, bass.ds(n, 1)], ACT.Square).then_inc(s_sqr, 1)
            act.wait_ge(s_n2, 2)
            act.activation(r_bc[:, 0:SEQ].rearrange("p (b n) -> p b n", b=2), ps[:, 6:8], ACT.Copy)
            act.activation(r_bc[:, SEQ:TOK], ps[:, 0, 64:64 + DEC], ACT.Copy).then_inc(s_rbc, 1)
            for n in range(KT):
                act.wait_ge(s_hn, n + 1)
                act.activation(h2_hi[:, n], hn[:, n % 2], ACT.Copy).then_inc(s_h2hi, 1)

            def mlp(g, last):
                for j in range(KT):
                    t = up_tile(g, j)
                    tile_done(act, t)
                    act.activation(chunks(relu), psum_set(t[1]), ACT.Relu).then_inc(s_free[t[1]], 1)
                    next_high(t)
                    act.wait_ge(s_fsq, KT * g + j + 1)
                    act.activation(ff_hi[:, j], act_sq[:], ACT.Copy).then_inc(s_ffhi, 1)
                for n in range(KT - 2 if last else KT):
                    next_high(down_tile(g, n))

            with act.Fori(0, FG - 1) as g:
                mlp(g, False)
            mlp(FG - 1, True)
            for t in range(NTT + 1):
                n = rows(t)
                act.wait_ge(s_yt, t + 1)
                need(act, s_ysq, t)
                b = 2 * (t % 4)
                act.activation(y_junk[0:n].rearrange("p (b n) -> p b n", b=2), ps[0:n, b:b + 2], ACT.Square,
                               accum_out=stat[0:n, t:t + 1]).then_inc(s_ysq, 1)

        @block.vector
        def _(dve):
            def split_qkv(hn):
                for q in range(WQ):
                    part = slice(2 * q, 2 * q + 2)
                    dve.wait_ge(s_whi, WQ * hn + q + 1)
                    dve.tensor_tensor(w_lo[:, :, part], w_raw[:, :, part], w_hi[:, :, part].bitcast(F32),
                                      ALU.subtract).then_inc(s_wlo, 1)

            def x_variance(t):
                n = rows(t)
                dve.wait_ge(s_sq, t + 1)
                dve.tensor_scalar(stat[0:n, 16 + t:17 + t], stat[0:n, t:t + 1], 1.0 / D, RMS_EPS, ALU.mult,
                                  ALU.add).then_inc(s_var, 1)

            def x_normed(t):
                n = rows(t)
                dve.wait_ge(s_rstd, t + 1)
                need(dve, s_ht, 2 * t - 2)
                dve.scalar_tensor_tensor(x_nrm[0:n, t % 2], x_in[0:n, t % 3], stat[0:n, 48 + t % 16:49 + t % 16],
                                         g_bc[0:n], ALU.mult, ALU.mult).then_inc(s_xn, 1)

            def h_low(t):
                n = rows(t)
                for r in range(2):
                    dve.wait_ge(s_hhi, 2 * t + r + 1)
                    dve.tensor_tensor(h_lo[:, 4 * r:4 * r + 4, toks(t)],
                                      bank_t[r][:, 0:4 * n].rearrange("p (k n) -> p k n", k=4),
                                      h_hi[:, 4 * r:4 * r + 4, toks(t)].bitcast(F32), ALU.subtract).then_inc(s_hlo, 1)

            def rotate(hp, par, t, k_par):
                n = rows(t)
                dve.wait_ge(s_z, 9 * hp + t + 1)
                need(dve, s_qk, 9 * hp + t)
                if t == 0:
                    need(dve, s_kv[par], 80 * k_par)
                z = bank_z[0:n, 0:2 * P].rearrange("p (m s d) -> p m s d", m=4, s=2)
                c4 = rope_c[0:n, t:t + 1, :].to_broadcast([n, 4, HALF])
                s4 = rope_s[0:n, t:t + 1, :].to_broadcast([n, 4, HALF])
                o_c = rc[0:n].rearrange("p (m s d) -> p m s d", m=4, s=2)
                o_s = rs[0:n].rearrange("p (m s d) -> p m s d", m=4, s=2)
                for s in range(2):
                    dve.tensor_tensor(o_c[:, :, s], z[:, :, s], c4, ALU.mult)
                dve.scalar_tensor_tensor(o_s[:, :, 0], z[:, :, 1], -1.0, s4, ALU.mult, ALU.mult)
                dve.tensor_tensor(o_s[:, :, 1], z[:, :, 0], s4, ALU.mult)
                dve.tensor_copy(kv_st[0:n, par, t, 1], bank_z[0:n, 2 * P:3 * P]).then_inc(s_zfree, 1)

            def qk_low(hp, par, t):
                dve.wait_ge(s_qkhi, 8 * hp + t + 1)
                dve.tensor_tensor(qk_lo[:, par, :, toks(t)], bank_t[1][:, 0:2 * P].rearrange("p (j n) -> p j n", j=2),
                                  qk_hi[:, par, :, toks(t)].bitcast(F32), ALU.subtract).then_inc(s_qklo, 1)

            def maximum(h, i, c):
                n = (i + 1) * P
                k = 16 * h + 2 * i + c + 1
                dve.wait_ge(s_s, k)
                dve.tensor_reduce(mx[:, i % 2, c:c + 1], bank_s[:, c, 0:n], AX_X, ALU.max).then_inc(s_mx, 1)
                dve.wait_ge(s_mx, k)
                need(dve, s_exp, k - 4)
                dve.tensor_scalar(nbias[:, i % 2, c:c + 1], mx[:, i % 2, c:c + 1], -SCALE, None,
                                  ALU.mult).then_inc(s_nb, 1)

            def weights(h, i):
                n = (i + 1) * P
                dve.wait_ge(s_exp, 16 * h + 2 * i + 2)
                dve.reciprocal(rsum[:, i], sums[:, i]).then_inc(s_rsum, 1)
                dve.wait_ge(s_rsum, 8 * h + i + 1)
                dve.scalar_tensor_tensor(ratio[:, i % 2:i % 2 + 1], sums[:, i, 0:1], nlam[:], rsum[:, i, 1:2],
                                         ALU.mult, ALU.mult).then_inc(s_ratio, 1)
                dve.wait_ge(s_ratio, 8 * h + i + 1)
                dve.scalar_tensor_tensor(prob[:, i % 2, 0, 0:n], prob[:, i % 2, 1, 0:n], ratio[:, i % 2:i % 2 + 1],
                                         prob[:, i % 2, 0, 0:n], ALU.mult, ALU.add).then_inc(s_a, 1)

            def weight_low(h, i, r):
                dve.wait_ge(s_athi, 12 * h + ROUNDS[i] + r + 1)
                n = min(512, (i + 1) * P - 512 * r)
                sl = slice(512 * r, 512 * r + n)
                dve.tensor_tensor(aT_lo[:, sl], bank_t[r][:, 0:n], aT_hi[:, sl].bitcast(F32),
                                  ALU.subtract).then_inc(s_atlo, 1)

            def o_sum(h, par, i):
                dve.wait_ge(s_ol, 8 * h + i + 1)
                dve.scalar_tensor_tensor(o_st[:, par, i], bank_o[:, 0:P], rsum[:, i, 0:1], o_low[:], ALU.mult,
                                         ALU.add).then_inc(s_oe, 1)

            def normed_head(h, par):
                dve.wait_ge(s_oq, 8 * h + 8)
                dve.tensor_scalar(o_var[:], ssq[:, par], 1.0 / DH, SUBLN_EPS, ALU.mult, ALU.add).then_inc(s_ovar, 1)
                dve.wait_ge(s_orstd, h + 1)
                dve.tensor_tensor(o_st[:, par], o_st[:, par], o_rstd[:].unsqueeze(2).to_broadcast([P, NTT, P]),
                                  ALU.mult).then_inc(s_on, 1)

            def head(h, par, proj, normed, k_par):
                if proj:
                    split_qkv(h + 1)
                for s in range(NTT + 1):
                    if s < NTT:
                        maximum(h, s, 0)
                        maximum(h, s, 1)
                    if normed and s == 1:
                        normed_head(h - 1, 1 - par)
                    if s >= 2:
                        o_sum(h, par, s - 2)
                    elif s == 0 and normed:
                        o_sum(h - 1, 1 - par, NTT - 1)
                    if s >= 1:
                        weight_low(h, s - 1, 0)
                        if proj:
                            qk_low(h + 1, 1 - par, s - 1)
                    if s < NTT:
                        weights(h, s)
                    if proj:
                        rotate(h + 1, 1 - par, s, k_par)
                    if s >= 5:
                        weight_low(h, s - 1, 1)

            split_qkv(0)
            dve.wait_ge(s_const, N_CONST)
            dve.tensor_copy(mask[:], mask_in[:])
            dve.tensor_copy(identb[:], ident[:]).then_inc(s_mask, 1)
            dve.tensor_tensor(lam_pr[:], lam_in[:, 0:4:2], lam_in[:, 1:4:2], ALU.mult).then_inc(s_lam_pr, 1)
            dve.wait_ge(s_lam_pr, 1)
            dve.tensor_reduce(stat[:, 32:34], lam_pr[:], AX_X, ALU.add).then_inc(s_lam_sum, 1)
            dve.wait_ge(s_lam_exp, 1)
            dve.tensor_tensor(stat[:, 36:37], stat[:, 35:36], stat[:, 34:35], ALU.subtract).then_inc(s_lam1, 1)
            dve.wait_ge(s_lam1, 1)
            dve.tensor_scalar(nlam[:], stat[:, 36:37], -LAM_INIT, None, ALU.add).then_inc(s_lam, 1)
            dve.wait_ge(s_lam, 1)
            for t in range(NTT + 5):
                if t <= NTT:
                    x_variance(t)
                if 1 <= t <= NTT + 1:
                    x_normed(t - 1)
                if 2 <= t <= NTT + 2:
                    h_low(t - 2)
                if 3 <= t <= NTT + 3:
                    rotate(0, 0, t - 3, 0)
                if 4 <= t < NTT + 4:
                    qk_low(0, 0, t - 4)
            head(0, 0, True, False, 0)
            with dve.Fori(0, HEADS // 2 - 1) as p:
                head(2 * p + 1, 1, True, True, p + 1)
                head(2 * p + 2, 0, True, True, p + 1)

            def low(l):
                dve.wait_ge(s_whi, W_QKV + l + 1)
                dve.tensor_tensor(w_lo[:, l], w_raw[:, l], w_hi[:, l].bitcast(F32), ALU.subtract).then_inc(s_wlo, 1)

            def next_low(t):
                sh, sp, lh, lp = t
                dve.wait_ge(s_whi, W_QKV + 2 * lh + lp + 3)
                dve.tensor_tensor(w_lo[:, lp], w_raw[:, lp], w_hi[:, lp].bitcast(F32), ALU.subtract).then_inc(s_wlo, 1)

            low(0)
            low(1)
            head(HEADS - 1, 1, False, True, 0)
            o_sum(HEADS - 1, 1, NTT - 1)
            normed_head(HEADS - 1, 1)
            attention_done(dve)

            def pooling(g):
                w = WINDOWS[g]
                done = sum(range(1, g + 1))
                src, reach = up, 1
                if g:
                    dve.wait_ge(s_pllo, g)
                for k in range(g + 1):
                    lo_ = 2 * reach - 1
                    if k:
                        dve.wait_ge(s_win, done + k)
                    dst_ = win[:, k % 2]
                    dve.tensor_tensor(dst_[:, lo_:PAD + SEQ], src[:, lo_:PAD + SEQ], src[:, lo_ - reach:PAD + SEQ - reach],
                                      ALU.add).then_inc(s_win, 1)
                    src, reach = dst_, 2 * reach
                dve.tensor_copy(us[:, g, :, BUF], up[:, PAD + SEQ:PAD + TOK]).then_inc(s_ufx, 1)
                dve.wait_ge(s_win, done + g + 1)
                dve.tensor_tensor(ufix[:, 0:w - 1], src[:, PAD:PAD + w - 1], inv_n[:, 0:w - 1], ALU.mult)
                dve.scalar_tensor_tensor(pooled[:, w - 1:SEQ], src[:, PAD + w - 1:PAD + SEQ], 1.0 / w,
                                         up[:, PAD + w - 1:PAD + SEQ], ALU.mult, ALU.subtract)
                if g == 0:
                    dve.wait_ge(s_us, 1)
                dve.wait_ge(s_ufx, 2 * g + 1)
                dve.tensor_reduce(ufix[:, 16:16 + DEC], us[:, g, :, 16 - w:16], AX_X, ALU.add).then_inc(s_ufx, 1)
                dve.wait_ge(s_ufx, 2 * g + 2)
                dve.scalar_tensor_tensor(pooled[:, SEQ:TOK], ufix[:, 16:16 + DEC], 1.0 / w, us[:, g, :, BUF], ALU.mult,
                                         ALU.subtract)
                dve.tensor_tensor(pooled[:, 0:w - 1], ufix[:, 0:w - 1], up[:, PAD:PAD + w - 1],
                                  ALU.subtract).then_inc(s_pooled, 1)

            def pooled_low(g):
                dve.wait_ge(s_plhi, g + 1)
                dve.tensor_tensor(pl_lo[:], pooled[:], pl_hi[:].bitcast(F32), ALU.subtract).then_inc(s_pllo, 1)

            def own_scores():
                dve.wait_ge(s_smp, 48)
                dve.tensor_tensor(smp[0:DEC, 3], smp[0:DEC, 0], smp[0:DEC, 1], ALU.mult).then_inc(s_own, 1)
                dve.wait_ge(s_own, 1)
                dve.tensor_reduce(own_s[0:DEC], smp[0:DEC, 3].rearrange("p (m e) -> p m e", e=HD), AX_X,
                                  ALU.add).then_inc(s_own, 1)
                dve.wait_ge(s_own, 2)
                dve.tensor_tensor(own[0:DEC], own_s[0:DEC].unsqueeze(1).to_broadcast([DEC, DEC, 16]),
                                  eye8[0:DEC].unsqueeze(2).to_broadcast([DEC, DEC, 16]), ALU.mult).then_inc(s_own, 1)

            def sum_keys(b):
                dve.wait_ge(s_pg[b % 2], 80 * (b // 2) + 80)
                dve.tensor_tensor(kv_pg[:, b % 2, PAGES - 1], kv_pg[:, b % 2, PAGES - 1], q_bc[b % 2][:],
                                  ALU.mult).then_inc(s_prod2, 1)
                dve.wait_ge(s_prod2, b + 1)
                dve.wait_ge(s_prod, b + 1)
                dve.tensor_reduce(sc_all[:, :, b * 16:(b + 1) * 16],
                                  kv_pg[:, b % 2].rearrange("p g (m e) -> p g m e", e=HD), AX_X,
                                  ALU.add).then_inc(s_kred, 1)

            def sample_softmax():
                dve.wait_ge(s_sct, 1)
                dve.wait_ge(s_vtc, 1)
                dve.tensor_reduce(dst[:, 0:1], ps[:, 6], AX_X, ALU.max).then_inc(s_soft, 1)
                dve.wait_ge(s_soft, 1)
                dve.tensor_tensor(dst[:, 1:2], dst[:, 0:1], dst[:, 8:9], ALU.max).then_inc(s_soft, 1)
                dve.wait_ge(s_soft, 2)
                dve.tensor_scalar(dst[:, 2:3], dst[:, 1:2], -SCALE, None, ALU.mult).then_inc(s_soft, 1)
                dve.wait_ge(s_sexp, 1)
                dve.tensor_tensor(dst[:, 5:6], dst[:, 3:4], dst[:, 4:5], ALU.add).then_inc(s_soft, 1)
                dve.wait_ge(s_soft, 4)
                dve.reciprocal(dst[:, 6:7], dst[:, 5:6])
                dve.scalar_tensor_tensor(dst[:, 7:8], cols[:, 15:16], nlam[:], cols[:, 14:15], ALU.mult,
                                         ALU.add).then_inc(s_soft, 1)
                dve.wait_ge(s_soft, 5)
                dve.tensor_tensor(dst[:, 9:10], dst[:, 7:8], dst[:, 6:7], ALU.mult).then_inc(s_soft, 1)
                dve.wait_ge(s_soft, 6)
                dve.tensor_scalar(sm_w[:], sm_w[:], dst[:, 9:10], None, ALU.mult).then_inc(s_soft, 1)
                dve.tensor_tensor(dst[:, 10:11], dst[:, 4:5], dst[:, 9:10], ALU.mult).then_inc(s_soft, 1)
                dve.wait_ge(s_soft, 8)
                dve.tensor_scalar(ones_a[:], ones[:], dst[:, 10:11], None, ALU.mult).then_inc(s_soft, 1)

            dve.wait_ge(s_ust, 1)
            dve.tensor_copy(us[:, :, :, 0:BUF], ps[:, 6, 0:NG * DEC * BUF].rearrange("p (g b r) -> p g b r", g=NG, b=DEC)
                            ).then_inc(s_us, 1)
            dve.wait_ge(s_in2, 64)
            for s_, kind, n, t in part_a():
                if kind == "u":
                    tile_out(dve, t)
                    pooling(n)
                    next_low(t)
                    if n == 0:
                        own_scores()
                        dve.wait_ge(s_wghi, 1)
                        dve.tensor_tensor(wg_lo[:], wg_raw[:], wg_hi[:].bitcast(F32), ALU.subtract).then_inc(s_wglo, 1)
                        pooled_low(0)
                elif kind == "grp":
                    tile_done(dve, t)
                    dve.wait_ge(s_yhi, n + 1)
                    dve.scalar_tensor_tensor(chunks(y_lo[:, n]), psum_set(t[1]), scale_c[:, n:n + 1],
                                             chunks(y_hi[:, n].bitcast(F32)), ALU.mult,
                                             ALU.subtract).then_inc(s_free[t[1]], 1)
                    if n < NG - 1:
                        pooled_low(n + 1)
                elif kind == "gate":
                    next_low(t)
                else:
                    tile_done(dve, t)
                    if n == 0:
                        dve.wait_ge(s_free[1], 4)
                    else:
                        dve.wait_ge(s_free[0], t[0] + 1)
                    dve.tensor_tensor(chunks(merged[:, n]), psum_set(t[1]), chunks(gate), ALU.mult).then_inc(s_free[t[1]], 1)
                    next_low(t)
                for b in range(DEC):
                    if REDUCE_AT[b] == s_:
                        sum_keys(b)
                if s_ == S_LOOP - 2:
                    sample_softmax()

            def pooled_tile(i):
                t = pool_tile(i)
                tile_done(dve, t)
                tile_out(dve, gate_tile(i))
                dve.tensor_tensor(merged[:, bass.ds(N_A + i, 1)].rearrange("p a (c n) -> p (a c) n", c=NCH), psum_set(1),
                                  chunks(gate), ALU.mult).then_inc(s_free[1], 1)
                next_low(t)

            def weigh_values(i, slot):
                b = 2 * i + slot
                dve.wait_ge(s_pg[slot], PG_K + 16 * PAGES * (i + 1))
                dve.tensor_tensor(*weighing(b, slot, 0), ALU.mult).then_inc(s_vs, 1)
                dve.wait_ge(s_vp, b + 1)
                dve.wait_ge(s_vs, VS * b + 1)
                dve.tensor_tensor(kv_pg[:, slot, 0:2], kv_pg[:, slot, 0:2], kv_pg[:, slot, 2:4], ALU.add).then_inc(s_vs, 1)
                dve.wait_ge(s_vs, VS * b + 2)
                dve.tensor_tensor(kv_pg[:, slot, 0], kv_pg[:, slot, 0], kv_pg[:, slot, 1], ALU.add).then_inc(s_vs, 1)

            dve.wait_ge(s_vout, 1)
            with dve.Fori(0, DEC // 2) as i:
                weigh_values(i, 0)
                next_low(gate_tile(i))
                weigh_values(i, 1)
                pooled_tile(i)
            for i in range(DEC // 2, KT - N_A):
                next_low(gate_tile(i))
                pooled_tile(i)
            dve.wait_ge(s_vout, 2)
            dve.wait_ge(s_v, DEC)
            v_bh = vT.rearrange("p (h b) -> p b h", h=HEADS)
            dve.tensor_tensor(o_s[:, 1].rearrange("p (b h) -> p b h", b=DEC), v_bh,
                              a_new.rearrange("p (b h) -> p b h", b=DEC), ALU.mult).then_inc(s_osq, 1)
            dve.wait_ge(s_osq, 1)
            dve.tensor_tensor(o_s[:, 0], ps[:, 6, 0:64], o_s[:, 1], ALU.add).then_inc(s_osq, 1)
            dve.wait_ge(s_osq, 2)
            dve.tensor_tensor(o_s[:, 2], o_s[:, 0], o_s[:, 0], ALU.mult).then_inc(s_osq, 1)
            dve.wait_ge(s_oss, 1)
            n_bh = DEC * HEADS
            dve.tensor_scalar(dst[0:n_bh, 16:17], bank_o[0:n_bh, 0:1], 1.0 / DH, SUBLN_EPS, ALU.mult,
                              ALU.add).then_inc(s_osv, 1)
            dve.wait_ge(s_osr, 1)
            dve.tensor_scalar(o_s[0:n_bh, 3], ident[0:n_bh, 0:n_bh], dst[0:n_bh, 17:18], None, ALU.mult).then_inc(s_osd, 1)
            dve.wait_ge(s_oss, 2)
            dve.scalar_tensor_tensor(o_raw[:, :, SEQ:TOK], o_s[:, 0].rearrange("p (b h) -> p h b", b=DEC), cols[:, 1:2],
                                     bank_o[:, 64:64 + n_bh].rearrange("p (b h) -> p h b", b=DEC), ALU.mult,
                                     ALU.mult).then_inc(s_osmp, 1)
            for h in range(HEADS):
                dve.wait_ge(s_ohi, h + 1)
                dve.tensor_tensor(o_lo[:, h], o_raw[:, h], o_hi[:, h].bitcast(F32), ALU.subtract).then_inc(s_olo, 1)

            def attention_tile(n):
                t = ap_tile(n)
                tile_done(dve, t)
                tile_out(dve, ga_tile(n))
                dve.tensor_tensor(chunks(gate), psum_set(1), chunks(gate), ALU.mult).then_inc(s_free[1], 1)
                tile_out(dve, t)
                m_n = merged[:, bass.ds(n, 1)]
                dve.tensor_tensor(m_n, m_n, gate[:].unsqueeze(1), ALU.add).then_inc(s_addm, 1)
                next_low(t)

            def merged_low(n):
                dve.wait_ge(s_mghi, n + 1)
                dve.tensor_tensor(mg_lo[:, n], merged[:, n], mg_hi[:, n].bitcast(F32), ALU.subtract).then_inc(s_mglo, 1)

            with dve.Fori(0, KT - 1) as n:
                next_low(ga_tile(n))
                attention_tile(n)
            next_low(ga_tile(KT - 1))
            for n in range(KT - 1):
                merged_low(n)
            attention_tile(KT - 1)
            merged_low(KT - 1)

            dve.wait_ge(s_addm, KT)
            dve.memset(sq_sum[:], 0.0).then_inc(s_sqs, 1)
            with dve.Fori(0, KT // 2) as m:
                for par in range(2):
                    n, t = 2 * m + par, out_tile(m, par)
                    tile_done(dve, t)
                    dve.wait_ge(s_xc, n + 2)
                    x_n = x1[:, bass.ds(n, 1)].rearrange("p a (c n) -> p (a c) n", c=NCH)
                    dve.tensor_tensor(x_n, psum_set(par), chunks(xT[:, par]), ALU.add).then_inc(s_free[par], 1)
                    next_low(t)
                    dve.wait_ge(s_sqr, n + 1)
                    dve.wait_ge(s_sqs, n + 1)
                    dve.tensor_tensor(sq_sum[:], sq_sum[:], sq[:], ALU.add).then_inc(s_sqs, 1)
            dve.wait_ge(s_n2, 1)
            dve.tensor_scalar(stat[:, 16:16 + NTT], ps[:, 0, 0:NTT], 1.0 / D, RMS_EPS, ALU.mult, ALU.add)
            dve.tensor_scalar(stat[0:DEC, 24:25], ps[0:DEC, 0, NTT:NTT + 1], 1.0 / D, RMS_EPS, ALU.mult,
                              ALU.add).then_inc(s_v2, 1)
            dve.wait_ge(s_r2, 1)
            dve.tensor_tensor(diag[:, 0:NTT], ident[:].unsqueeze(1).to_broadcast([P, NTT, P]),
                              stat[:, 48:48 + NTT].unsqueeze(2).to_broadcast([P, NTT, P]), ALU.mult)
            dve.tensor_scalar(diag[0:DEC, NTT, 0:DEC], ident[0:DEC, 0:DEC], stat[0:DEC, 56:57], None,
                              ALU.mult).then_inc(s_diag, 1)
            dve.wait_ge(s_rbc, 1)
            for n in range(KT + 1):
                if n < KT:
                    need(dve, s_h2lo, n - 1)
                    dve.scalar_tensor_tensor(hn[:, n % 2], x1[:, n], g_mlp_c[:, n:n + 1], r_bc[:], ALU.mult,
                                             ALU.mult).then_inc(s_hn, 1)
                if n:
                    dve.wait_ge(s_h2hi, n)
                    dve.tensor_tensor(h2_lo[:, n - 1], hn[:, (n - 1) % 2], h2_hi[:, n - 1].bitcast(F32),
                                      ALU.subtract).then_inc(s_h2lo, 1)

            def mlp(g, last):
                for j in range(KT):
                    t = up_tile(g, j)
                    tile_out(dve, t)
                    if j:
                        dve.wait_ge(s_fflo, KT * g + j)
                    dve.tensor_tensor(act_sq[:], relu[:], relu[:], ALU.mult).then_inc(s_fsq, 1)
                    dve.wait_ge(s_ffhi, KT * g + j + 1)
                    dve.tensor_tensor(ff_lo[:, j], act_sq[:], ff_hi[:, j].bitcast(F32), ALU.subtract).then_inc(s_fflo, 1)
                    next_low(t)
                for n in range(KT):
                    t = down_tile(g, n)
                    tile_done(dve, t)
                    dve.wait_ge(s_free[t[1]], t[0])
                    dve.tensor_tensor(x1_chunks[:, n], psum_set(t[1]), x1_chunks[:, n], ALU.add).then_inc(s_free[t[1]], 1)
                    if not (last and n >= KT - 2):
                        next_low(t)

            with dve.Fori(0, FG - 1) as g:
                mlp(g, False)
            mlp(FG - 1, True)
            dve.wait_ge(s_gf, 16)
            for t in range(NTT + 2):
                if t <= NTT:
                    n = rows(t)
                    dve.wait_ge(s_ysq, t + 1)
                    dve.tensor_scalar(stat[0:n, 16 + t:17 + t], stat[0:n, t:t + 1], 1.0 / D, RMS_EPS, ALU.mult,
                                      ALU.add).then_inc(s_yv, 1)
                if t:
                    q = t - 1
                    n = rows(q)
                    dve.wait_ge(s_yr, q + 1)
                    need(dve, s_yst[q % 2], 16 * (q // 2))
                    dve.scalar_tensor_tensor(y_st[0:n, q % 2].rearrange("p (b n) -> p b n", b=2),
                                             ps[0:n, 2 * (q % 4):2 * (q % 4) + 2], stat[0:n, 48 + q % 16:49 + q % 16],
                                             gf_bc[0:n].rearrange("p (b n) -> p b n", b=2), ALU.mult,
                                             ALU.mult).then_inc(s_yo, 1)

        @block.gpsimd
        def _(pool):
            def rstd_x(t):
                n = rows(t)
                pool.wait_ge(s_var, t + 1)
                pool.tensor_tensor(stat[0:n, 48 + t % 16:49 + t % 16], stat[0:n, 16 + t:17 + t], half_neg[0:n, 0:1],
                                   ALU.pow).then_inc(s_rstd, 1)

            def rotated(hp, par, t):
                n = rows(t)
                pool.wait_ge(s_zfree, 9 * hp + t + 1)
                if t < NTT:
                    need(pool, s_qkt, 8 * hp + t)
                    q_out = q_nat[:]
                else:
                    q_out = qs_st[0:n, par]
                pool.tensor_tensor(q_out, rc[0:n, 0:P], rs[0:n, 0:P], ALU.add)
                pool.tensor_tensor(kv_st[0:n, par, t, 0], rc[0:n, P:2 * P], rs[0:n, P:2 * P], ALU.add).then_inc(s_qk, 1)
                if t < NTT:
                    pool.wait_ge(s_vhi, 8 * hp + t + 1)
                    pool.tensor_tensor(v_hl[:, par, t, 1], kv_st[:, par, t, 1], v_hl[:, par, t, 0].bitcast(F32),
                                       ALU.subtract).then_inc(s_vlo, 1)

            def head(h, par, proj, normed):
                for s in range(NTT + 1):
                    if normed and s == 1:
                        rstd_head(h - 1)
                    if proj:
                        rotated(h + 1, 1 - par, s)

            def rstd_head(h):
                pool.wait_ge(s_ovar, h + 1)
                pool.tensor_tensor(o_rstd[:], o_var[:], half_neg[:, 0:NTT], ALU.pow).then_inc(s_orstd, 1)

            pool.memset(half_neg[:], -0.5).then_inc(s_half, 1)
            pool.memset(ones[:], 1.0).then_inc(s_ones, 1)
            pool.wait_ge(s_half, 1)
            for t in range(NTT + 4):
                if t <= NTT:
                    rstd_x(t)
                if t >= 3:
                    rotated(0, 0, t - 3)
            head(0, 0, True, False)
            with pool.Fori(0, HEADS // 2 - 1) as p:
                head(2 * p + 1, 1, True, True)
                head(2 * p + 2, 0, True, True)
            head(HEADS - 1, 1, False, True)
            rstd_head(HEADS - 1)
            attention_done(pool)
            pool.memset(up[:, 0:PAD], 0.0).then_inc(s_pad, 1)
            for b in range(DEC):
                pool.wait_ge(s_pg[b % 2], 80 * (b // 2) + 80)
                part = kv_pg[:, b % 2, 0:PAGES - 1]
                pool.tensor_tensor(part, part, q_bc[b % 2][:].unsqueeze(1).to_broadcast([P, PAGES - 1, D]),
                                   ALU.mult).then_inc(s_prod, 1)
            pool.wait_ge(s_vout, 1)
            with pool.Fori(0, DEC // 2) as i:
                for slot in range(2):
                    pool.wait_ge(s_pg[slot], PG_K + 16 * PAGES * (i + 1))
                    pool.tensor_tensor(*weighing(2 * i + slot, slot, PAGES // 2), ALU.mult).then_inc(s_vp, 1)
            pool.wait_ge(s_osv, 1)
            n_bh = DEC * HEADS
            pool.tensor_tensor(dst[0:n_bh, 17:18], dst[0:n_bh, 16:17], half_neg[0:n_bh, 0:1], ALU.pow).then_inc(s_osr, 1)
            pool.wait_ge(s_v2, 1)
            pool.tensor_tensor(stat[:, 48:48 + NTT], stat[:, 16:16 + NTT], half_neg[:, 0:NTT], ALU.pow)
            pool.tensor_tensor(stat[0:DEC, 56:57], stat[0:DEC, 24:25], half_neg[0:DEC, 0:1], ALU.pow).then_inc(s_r2, 1)
            for t in range(NTT + 1):
                n = rows(t)
                pool.wait_ge(s_yv, t + 1)
                pool.tensor_tensor(stat[0:n, 48 + t % 16:49 + t % 16], stat[0:n, 16 + t:17 + t], half_neg[0:n, 0:1],
                                   ALU.pow).then_inc(s_yr, 1)


def constants():
    import numpy as np

    inv_freq = (10000.0 ** (-np.arange(HALF) * (2.0 / HD))).astype(np.float32)
    pos = np.arange((NTT + 1) * P, dtype=np.float32)
    pos[SEQ:] = PAST
    ang = (pos[:, None] * inv_freq[None, :]).astype(np.float32)
    table = lambda a: np.ascontiguousarray(a.astype(np.float32).reshape(NTT + 1, P, HALF).transpose(1, 0, 2))
    q = np.arange(P)
    mask = np.zeros((P, P), np.float32)
    mask[q[:, None] < q[None, :]] = -1e30
    k = np.arange(P)
    cols = np.zeros((P, 32), np.float32)
    cols[:, 14], cols[:, 15] = k % 2 == 0, k % 2 == 1
    return {
        "c_cos": table(np.cos(ang)),
        "c_sin": table(np.sin(ang)),
        "c_ident": np.eye(P, dtype=np.float32),
        "c_mask": mask,
        "c_cols": cols,
        "c_sel": (k[:, None] // 2 == np.arange(P // 2)[None]).astype(np.float32),
        "c_eye8": np.eye(DEC, dtype=np.float32),
        "c_inv": np.tile((1.0 / np.arange(1, 17)).astype(np.float32), (P, 1)),
    }


OUTS = [(1, SEQ, D), (DEC, 1, D), (1, 1, SEQ, HEADS, DH), (1, 1, SEQ, HEADS, DH), (1, 1, BUF, D_POOL),
        (1, DEC, 1, HEADS, DH), (1, DEC, 1, HEADS, DH), (1, DEC, BUF, D_POOL)]
INS = ["x_prompt", "x_sample", "state_pool", "cache_k", "cache_v", "page_table", "g_mix", "w_in", "w_pool_grp",
       "pool_scale", "w_pool_proj", "lambda_q1", "lambda_k1", "lambda_q2", "lambda_k2", "g_subln", "w_attn_proj",
       "w_o", "g_mlp", "w_up", "w_down", "g_final"]


def kernel(**inputs):
    import concourse.bacc as bacc
    import numpy as np
    from concourse.bass_utils import run_bass_kernel_spmd

    nc = bacc.Bacc("TRN2", target_bir_lowering=False, num_devices=1, dynamic_dma_scratch_size=1024)
    arrays = {name: np.ascontiguousarray(inputs[name]) for name in INS}
    arrays.update(constants())
    arrays = {f"in_{name}": a for name, a in arrays.items()}
    ins = [nc.dram_tensor(name, a.shape, mybir.dt.from_np(a.dtype), kind="ExternalInput").ap()
           for name, a in arrays.items()]
    outs = [nc.dram_tensor(f"out_{i}", shape, F32, kind="ExternalOutput").ap() for i, shape in enumerate(OUTS)]
    decoder_layer(nc, ins, outs)
    r = run_bass_kernel_spmd(nc, [arrays], core_ids=[0])
    return tuple(r.results[0][f"out_{i}"] for i in range(len(OUTS)))
```
